# Optimizing a Trainium2 kernel written in Bass

```python
import jax, jax.numpy as jnp
from jax import lax
import numpy as np

D_MODEL = 1024
BATCH = 1
SEQ = 2048
DEPTH = 1

HEAD_DIM = 64
RWKV_HEADS = 8
RWKV_WIDTH = RWKV_HEADS * HEAD_DIM
DECAY_LORA = 32
AAA_LORA = 32
ATTN_HEADS = 8
ATTN_WIDTH = ATTN_HEADS * HEAD_DIM
MIX_WIDTH = RWKV_WIDTH + ATTN_WIDTH
Q_RANK = 256
KV_RANK = 128
IDX_HEADS = 4
IDX_DIM = 64
TOPK_MAX = 256
Q_BLOCK = 128
NORM_EPS = 1e-6
LN_EPS = 1e-5
GN_EPS = 64e-5

SHIFT_SIZES = [RWKV_WIDTH, RWKV_WIDTH, RWKV_WIDTH, DECAY_LORA, AAA_LORA]
SHIFT_COLS = sum(SHIFT_SIZES)
IN_SIZES = [SHIFT_COLS, RWKV_WIDTH, Q_RANK, KV_RANK, IDX_DIM, IDX_HEADS, ATTN_WIDTH]
IN_COLS = sum(IN_SIZES)
SHIFT_SPLITS = np.cumsum(SHIFT_SIZES)[:-1].tolist()
IN_SPLITS = np.cumsum(IN_SIZES)[:-1].tolist()


def rmsnorm(x, g):
    xf = x.astype(jnp.float32)
    y = xf * lax.rsqrt(jnp.mean(xf * xf, axis=-1, keepdims=True) + NORM_EPS)
    return (y * g.astype(jnp.float32)).astype(x.dtype)

def layernorm(x, g, b):
    xf = x.astype(jnp.float32)
    mu = jnp.mean(xf, axis=-1, keepdims=True)
    var = jnp.mean(jnp.square(xf - mu), axis=-1, keepdims=True)
    y = (xf - mu) * lax.rsqrt(var + LN_EPS)
    return (y * g.astype(jnp.float32) + b.astype(jnp.float32)).astype(x.dtype)

def rwkv7_scan(r, decay, k, v, kk, a):
    B, T, H, D = r.shape
    tm = lambda t: jnp.moveaxis(t, 1, 0)

    def step(S, inp):
        r_t, w_t, k_t, v_t, kk_t, a_t = inp
        sa = jnp.einsum('bhij,bhj->bhi', S, -kk_t)
        S = (S * w_t[:, :, None, :]
             + sa[..., None] * (kk_t * a_t)[:, :, None, :]
             + v_t[..., None] * k_t[:, :, None, :])
        return S, jnp.einsum('bhij,bhj->bhi', S, r_t)

    S0 = jnp.zeros((B, H, D, D), jnp.float32)
    _, y = lax.scan(step, S0, (tm(r), tm(decay), tm(k), tm(v), tm(kk), tm(a)))
    return jnp.moveaxis(y, 0, 1)

def rwkv7_branch(p_shift, gate, mu_shift, w0, w_up, a0, a_up, k_k, k_a, r_k, gn_g, gn_b):
    B, T, _ = p_shift.shape
    f32 = jnp.float32
    prev = jnp.pad(p_shift, ((0, 0), (1, 0), (0, 0)))[:, :-1]
    xs = p_shift + (prev - p_shift) * mu_shift
    r, k, v, wd, ad = jnp.split(xs, SHIFT_SPLITS, axis=-1)
    wlog = -jax.nn.softplus(-(w0 + jnp.tanh(wd) @ w_up)) - 0.5
    decay = jnp.exp(-jnp.exp(wlog.astype(f32)))
    a = jax.nn.sigmoid((a0 + ad @ a_up).astype(f32))
    heads = lambda t: t.astype(f32).reshape(B, T, RWKV_HEADS, HEAD_DIM)
    r, k, v, a, decay = heads(r), heads(k), heads(v), heads(a), heads(decay)
    kk = k * k_k.astype(f32)
    kk = kk / jnp.maximum(jnp.sqrt(jnp.sum(kk * kk, axis=-1, keepdims=True)), 1e-12)
    k = k * (1.0 + (a - 1.0) * k_a.astype(f32))
    y = rwkv7_scan(r, decay, k, v, kk, a)
    mu = jnp.mean(y, axis=-1, keepdims=True)
    var = jnp.mean(jnp.square(y - mu), axis=-1, keepdims=True)
    y = (y - mu) * lax.rsqrt(var + GN_EPS) * gn_g.astype(f32) + gn_b.astype(f32)
    y = y + jnp.sum(r * k * r_k.astype(f32), axis=-1, keepdims=True) * v
    y = y.reshape(B, T, RWKV_WIDTH).astype(gate.dtype)
    return y * jax.nn.silu(gate)

def dsa_branch(q_down, kv_down, k_idx_raw, w_idx, gate, q_norm_g, kv_norm_g,
               w_uq, w_uk, w_uv, w_qidx, kidx_g, kidx_b):
    B, T, _ = q_down.shape
    f32 = jnp.float32
    c_q = rmsnorm(q_down, q_norm_g)
    c_kv = rmsnorm(kv_down, kv_norm_g)
    q = (c_q @ w_uq).reshape(B, T, ATTN_HEADS, HEAD_DIM)
    q_abs = jnp.einsum('bthd,hrd->bthr', q, w_uk) * (HEAD_DIM ** -0.5)
    q_idx = (c_q @ w_qidx).reshape(B, T, IDX_HEADS, IDX_DIM)
    k_idx = layernorm(k_idx_raw, kidx_g, kidx_b).astype(f32)
    w_i = w_idx * (IDX_HEADS ** -0.5)
    topk = min(TOPK_MAX, T // 4)
    nb = T // Q_BLOCK
    blocks = lambda t: jnp.moveaxis(t.reshape(B, nb, Q_BLOCK, *t.shape[2:]), 1, 0)
    key_pos = jnp.arange(T)

    def attend(args):
        qa, qi, wi, t0 = args
        q_pos = t0 + jnp.arange(Q_BLOCK)
        causal = key_pos[None, :] <= q_pos[:, None]
        logits = jnp.einsum('bqhd,bsd->bqhs', qi.astype(f32), k_idx)
        score = jnp.einsum('bqh,bqhs->bqs', wi.astype(f32), jax.nn.relu(logits))
        score = jnp.where(causal[None], score, -jnp.inf)
        _, idx = lax.top_k(score, topk)
        c_sel = jax.vmap(lambda c, i: c[i])(c_kv, idx).astype(f32)
        valid = idx <= q_pos[None, :, None]
        s = jnp.einsum('bqhr,bqkr->bhqk', qa.astype(f32), c_sel)
        s = jnp.where(valid[:, None], s, -jnp.inf)
        p = jax.nn.softmax(s, axis=-1)
        return jnp.einsum('bhqk,bqkr->bqhr', p, c_sel)

    o_lat = lax.map(attend, (blocks(q_abs), blocks(q_idx), blocks(w_i), jnp.arange(nb) * Q_BLOCK))
    o_lat = jnp.moveaxis(o_lat, 0, 1).reshape(B, T, ATTN_HEADS, KV_RANK).astype(gate.dtype)
    o = jnp.einsum('bthr,hrd->bthd', o_lat, w_uv).reshape(B, T, ATTN_WIDTH)
    return o * jax.nn.silu(gate)

def hybrid_layer(x, norm_g, w_in, mu_shift, w0, w_up, a0, a_up, k_k, k_a, r_k, gn_g, gn_b,
                 q_norm_g, kv_norm_g, w_uq, w_uk, w_uv, w_qidx, kidx_g, kidx_b, w_out):
    xn = rmsnorm(x, norm_g)
    p = xn @ w_in
    p_shift, g_rwkv, q_down, kv_down, k_idx_raw, w_idx, g_attn = jnp.split(p, IN_SPLITS, axis=-1)
    y_rwkv = rwkv7_branch(p_shift, g_rwkv, mu_shift, w0, w_up, a0, a_up, k_k, k_a, r_k, gn_g, gn_b)
    y_attn = dsa_branch(q_down, kv_down, k_idx_raw, w_idx, g_attn, q_norm_g, kv_norm_g,
                        w_uq, w_uk, w_uv, w_qidx, kidx_g, kidx_b)
    y = jnp.concatenate([y_rwkv, y_attn], axis=-1) @ w_out
    return x + y

def first_inputs(seed: int = 0) -> dict:
    key = jax.random.key(seed)
    ks = jax.random.split(key, 24)
    L = DEPTH
    f32 = jnp.float32
    nrm = lambda k, shape, scale: scale * jax.random.normal(k, shape, f32)
    gain = lambda k, shape: 1.0 + 0.05 * jax.random.normal(k, shape, f32)
    hd = (L, RWKV_HEADS, HEAD_DIM)
    return {
        "x": nrm(ks[0], (BATCH, SEQ, D_MODEL), 1.0),
        "norm_g": gain(ks[1], (L, D_MODEL)),
        "w_in": nrm(ks[2], (L, D_MODEL, IN_COLS), D_MODEL ** -0.5),
        "mu_shift": jax.random.uniform(ks[3], (L, SHIFT_COLS), f32),
        "w0": jax.random.uniform(ks[4], (L, RWKV_WIDTH), f32, -2.0, 2.0),
        "w_up": nrm(ks[5], (L, DECAY_LORA, RWKV_WIDTH), 0.5 * DECAY_LORA ** -0.5),
        "a0": nrm(ks[6], (L, RWKV_WIDTH), 0.5),
        "a_up": nrm(ks[7], (L, AAA_LORA, RWKV_WIDTH), 0.5 * AAA_LORA ** -0.5),
        "k_k": 0.85 + 0.05 * jax.random.normal(ks[8], hd, f32),
        "k_a": gain(ks[9], hd),
        "r_k": nrm(ks[10], hd, 0.1),
        "gn_g": gain(ks[11], hd),
        "gn_b": nrm(ks[12], hd, 0.02),
        "q_norm_g": gain(ks[13], (L, Q_RANK)),
        "kv_norm_g": gain(ks[14], (L, KV_RANK)),
        "w_uq": nrm(ks[15], (L, Q_RANK, ATTN_WIDTH), Q_RANK ** -0.5),
        "w_uk": nrm(ks[16], (L, ATTN_HEADS, KV_RANK, HEAD_DIM), KV_RANK ** -0.5),
        "w_uv": nrm(ks[17], (L, ATTN_HEADS, KV_RANK, HEAD_DIM), KV_RANK ** -0.5),
        "w_qidx": nrm(ks[18], (L, Q_RANK, IDX_HEADS * IDX_DIM), Q_RANK ** -0.5),
        "kidx_g": gain(ks[19], (L, IDX_DIM)),
        "kidx_b": nrm(ks[20], (L, IDX_DIM), 0.02),
        "w_out": nrm(ks[21], (L, MIX_WIDTH, D_MODEL), MIX_WIDTH ** -0.5),
        "final_g": gain(ks[22], (D_MODEL,)),
    }

def first_block(x, norm_g, w_in, mu_shift, w0, w_up, a0, a_up, k_k, k_a, r_k, gn_g, gn_b,
              q_norm_g, kv_norm_g, w_uq, w_uk, w_uv, w_qidx, kidx_g, kidx_b, w_out, final_g):
    for l in range(DEPTH):
        x = hybrid_layer(x, norm_g[l], w_in[l], mu_shift[l], w0[l], w_up[l], a0[l], a_up[l],
                         k_k[l], k_a[l], r_k[l], gn_g[l], gn_b[l], q_norm_g[l], kv_norm_g[l],
                         w_uq[l], w_uk[l], w_uv[l], w_qidx[l], kidx_g[l], kidx_b[l], w_out[l])
    return rmsnorm(x, final_g)


N_MIXERS = 2
N_MEM = 256
MIX_WIDTH_2 = D_MODEL
MEM_HEADS = 4
MEM_WIDTH = MIX_WIDTH_2 // 4
MEM_HEAD_DIM = MEM_WIDTH // MEM_HEADS
MAIN_WIDTH = MIX_WIDTH_2 - MEM_WIDTH
MLA_HEADS = 12
QK_NOPE = 64
QK_ROPE = 32
V_HEAD = MAIN_WIDTH // MLA_HEADS
Q_LORA = (3 * D_MODEL) // 8
KV_LORA = D_MODEL // 4
ROPE_THETA = 10000.0
FNET_GROUPS = 4
FNET_GROUP_DIM = MAIN_WIDTH // FNET_GROUPS
EPS = 1e-6

MLA_IN = Q_LORA + KV_LORA + QK_ROPE + MEM_WIDTH + MIX_WIDTH_2
FNET_IN = MAIN_WIDTH + MEM_WIDTH + MIX_WIDTH_2


def rmsnorm_2(x, g):
    xf = x.astype(jnp.float32)
    y = xf * lax.rsqrt(jnp.mean(xf * xf, axis=-1, keepdims=True) + EPS)
    return (y * g.astype(jnp.float32)).astype(x.dtype)

def rope_tables(positions):
    inv_freq = 1.0 / (ROPE_THETA ** (jnp.arange(0, QK_ROPE, 2, dtype=jnp.float32) / QK_ROPE))
    ang = positions.astype(jnp.float32)[..., None] * inv_freq
    return jnp.cos(ang), jnp.sin(ang)

def apply_rope(t, cos, sin):
    tf = t.astype(jnp.float32)
    t1, t2 = tf[..., : QK_ROPE // 2], tf[..., QK_ROPE // 2:]
    return jnp.concatenate([t1 * cos - t2 * sin, t2 * cos + t1 * sin], axis=-1).astype(t.dtype)

def mla_attention(q_nope, q_rope, k_nope, k_rope, v):
    B, S, H, _ = q_nope.shape
    nb = S // Q_BLOCK
    scale = 1.0 / float(np.sqrt(QK_NOPE + QK_ROPE))

    def to_blocks(t):
        return jnp.moveaxis(t.reshape((B, nb, Q_BLOCK) + t.shape[2:]), 1, 0)

    def one_block(args):
        qn, qr = args
        s = (jnp.einsum('bqhd,bkhd->bhqk', qn, k_nope)
             + jnp.einsum('bqhr,bkr->bhqk', qr, k_rope)).astype(jnp.float32) * scale
        p = jax.nn.softmax(s, axis=-1).astype(v.dtype)
        return jnp.einsum('bhqk,bkhd->bqhd', p, v)

    out = lax.map(one_block, (to_blocks(q_nope), to_blocks(q_rope)))
    return jnp.moveaxis(out, 0, 1).reshape(B, S, H * V_HEAD)

def memory_cross_attention(q_mem, mem, mem_norm_g, w_mem_kv):
    B, S, _ = q_mem.shape
    q = q_mem.reshape(B, S, MEM_HEADS, MEM_HEAD_DIM)
    kv = (rmsnorm_2(mem, mem_norm_g) @ w_mem_kv).reshape(B, mem.shape[1], 2, MEM_HEADS, MEM_HEAD_DIM)
    k, v = kv[:, :, 0], kv[:, :, 1]
    s = jnp.einsum('bshd,bmhd->bhsm', q, k).astype(jnp.float32) * (1.0 / float(np.sqrt(MEM_HEAD_DIM)))
    p = jax.nn.softmax(s, axis=-1).astype(v.dtype)
    return jnp.einsum('bhsm,bmhd->bshd', p, v).reshape(B, S, MEM_WIDTH)

def mla_layer(x, mem, cos, sin, norm_g, w_in, q_norm_g, kv_norm_g, w_uq, w_ukv,
              mem_norm_g, w_mem_kv, w_out):
    B, S, _ = x.shape
    h = rmsnorm_2(x, norm_g)
    proj = h @ w_in
    o1 = Q_LORA
    o2 = o1 + KV_LORA
    o3 = o2 + QK_ROPE
    o4 = o3 + MEM_WIDTH
    c_q, c_kv, k_rope = proj[..., :o1], proj[..., o1:o2], proj[..., o2:o3]
    q_mem, gate = proj[..., o3:o4], proj[..., o4:]
    q = (rmsnorm_2(c_q, q_norm_g) @ w_uq).reshape(B, S, MLA_HEADS, QK_NOPE + QK_ROPE)
    kv = (rmsnorm_2(c_kv, kv_norm_g) @ w_ukv).reshape(B, S, MLA_HEADS, QK_NOPE + V_HEAD)
    q_nope = q[..., :QK_NOPE]
    q_rope = apply_rope(q[..., QK_NOPE:], cos[:, :, None, :], sin[:, :, None, :])
    k_nope, v = kv[..., :QK_NOPE], kv[..., QK_NOPE:]
    k_rope = apply_rope(k_rope, cos, sin)
    attn = mla_attention(q_nope, q_rope, k_nope, k_rope, v)
    mem_out = memory_cross_attention(q_mem, mem, mem_norm_g, w_mem_kv)
    branch = jnp.concatenate([attn, mem_out], axis=-1) * jax.nn.silu(gate)
    return x + branch @ w_out

def fnet_layer(x, mem, norm_g, w_in, w_fnet, mem_norm_g, w_mem_kv, w_out):
    B, S, _ = x.shape
    h = rmsnorm_2(x, norm_g)
    proj = h @ w_in
    f = proj[..., :MAIN_WIDTH].reshape(B, S, FNET_GROUPS, FNET_GROUP_DIM).astype(jnp.float32)
    q_mem = proj[..., MAIN_WIDTH:MAIN_WIDTH + MEM_WIDTH]
    gate = proj[..., MAIN_WIDTH + MEM_WIDTH:]
    spec = jnp.fft.fft2(f, axes=(1, 3), norm='ortho').real
    mixed = jnp.einsum('bsgc,gcd->bsgd', spec, w_fnet.astype(jnp.float32))
    mixed = mixed.reshape(B, S, MAIN_WIDTH).astype(x.dtype)
    mem_out = memory_cross_attention(q_mem, mem, mem_norm_g, w_mem_kv)
    branch = jnp.concatenate([mixed, mem_out], axis=-1) * jax.nn.silu(gate)
    return x + branch @ w_out

def second_inputs(seed: int = 0) -> dict:
    key = jax.random.key(seed)
    ks = jax.random.split(key, 24)
    f32 = jnp.float32

    def w(k, shape, fan_in):
        return jax.random.normal(k, shape, f32) * (fan_in ** -0.5)

    def gain(k, n):
        return 1.0 + 0.02 * jax.random.normal(k, (n,), f32)

    x = jax.random.normal(ks[0], (BATCH, SEQ, D_MODEL), f32)
    mem = jax.random.normal(ks[1], (BATCH, N_MEM, D_MODEL), f32)
    offsets = jax.random.randint(ks[2], (BATCH, 1), 0, 1024, dtype=jnp.int32)
    positions = (jnp.arange(SEQ, dtype=jnp.int32)[None, :] + offsets).astype(jnp.int32)
    return {
        "x": x,
        "mem": mem,
        "positions": positions,
        "norm_g_l0": gain(ks[3], D_MODEL),
        "w_in_l0": w(ks[4], (D_MODEL, MLA_IN), D_MODEL),
        "q_norm_g_l0": gain(ks[5], Q_LORA),
        "kv_norm_g_l0": gain(ks[6], KV_LORA),
        "w_uq_l0": w(ks[7], (Q_LORA, MLA_HEADS * (QK_NOPE + QK_ROPE)), Q_LORA),
        "w_ukv_l0": w(ks[8], (KV_LORA, MLA_HEADS * (QK_NOPE + V_HEAD)), KV_LORA),
        "mem_norm_g_l0": gain(ks[9], D_MODEL),
        "w_mem_kv_l0": w(ks[10], (D_MODEL, 2 * MEM_WIDTH), D_MODEL),
        "w_out_l0": w(ks[11], (MIX_WIDTH_2, D_MODEL), MIX_WIDTH_2),
        "norm_g_l1": gain(ks[12], D_MODEL),
        "w_in_l1": w(ks[13], (D_MODEL, FNET_IN), D_MODEL),
        "w_fnet_l1": w(ks[14], (FNET_GROUPS, FNET_GROUP_DIM, FNET_GROUP_DIM), FNET_GROUP_DIM),
        "mem_norm_g_l1": gain(ks[15], D_MODEL),
        "w_mem_kv_l1": w(ks[16], (D_MODEL, 2 * MEM_WIDTH), D_MODEL),
        "w_out_l1": w(ks[17], (MIX_WIDTH_2, D_MODEL), MIX_WIDTH_2),
        "final_norm_g": gain(ks[18], D_MODEL),
    }

def second_block(x, mem, positions,
              norm_g_l0, w_in_l0, q_norm_g_l0, kv_norm_g_l0, w_uq_l0, w_ukv_l0,
              mem_norm_g_l0, w_mem_kv_l0, w_out_l0,
              norm_g_l1, w_in_l1, w_fnet_l1, mem_norm_g_l1, w_mem_kv_l1, w_out_l1,
              final_norm_g):
    cos, sin = rope_tables(positions)
    for i in range(DEPTH):
        if i % N_MIXERS == 0:
            x = mla_layer(x, mem, cos, sin, norm_g_l0, w_in_l0, q_norm_g_l0, kv_norm_g_l0,
                          w_uq_l0, w_ukv_l0, mem_norm_g_l0, w_mem_kv_l0, w_out_l0)
        else:
            x = fnet_layer(x, mem, norm_g_l1, w_in_l1, w_fnet_l1,
                           mem_norm_g_l1, w_mem_kv_l1, w_out_l1)
    return rmsnorm_2(x, final_norm_g)


def setup_inputs(seed=0):
    out = dict(first_inputs(seed))
    for name, value in second_inputs(seed + 1).items():
        if name != "x":
            out[name + "_2"] = value
    return out


def reference(
    x, norm_g, w_in, mu_shift, w0, w_up, a0, a_up, k_k, k_a, r_k, gn_g, gn_b, q_norm_g,
    kv_norm_g, w_uq, w_uk, w_uv, w_qidx, kidx_g, kidx_b, w_out, final_g, mem_2, positions_2,
    norm_g_l0_2, w_in_l0_2, q_norm_g_l0_2, kv_norm_g_l0_2, w_uq_l0_2, w_ukv_l0_2,
    mem_norm_g_l0_2, w_mem_kv_l0_2, w_out_l0_2, norm_g_l1_2, w_in_l1_2, w_fnet_l1_2,
    mem_norm_g_l1_2, w_mem_kv_l1_2, w_out_l1_2, final_norm_g_2,
):
    x = first_block(
        x, norm_g, w_in, mu_shift, w0, w_up, a0, a_up, k_k, k_a, r_k, gn_g, gn_b, q_norm_g,
        kv_norm_g, w_uq, w_uk, w_uv, w_qidx, kidx_g, kidx_b, w_out, final_g,
    )
    return second_block(
        x, mem_2, positions_2, norm_g_l0_2, w_in_l0_2, q_norm_g_l0_2, kv_norm_g_l0_2, w_uq_l0_2,
        w_ukv_l0_2, mem_norm_g_l0_2, w_mem_kv_l0_2, w_out_l0_2, norm_g_l1_2, w_in_l1_2,
        w_fnet_l1_2, mem_norm_g_l1_2, w_mem_kv_l1_2, w_out_l1_2, final_norm_g_2,
    )


_drawn_inputs = setup_inputs


def setup_inputs(seed=0):
    import zlib

    import numpy as np

    out = dict(_drawn_inputs(seed))
    spreads = {}
    factors = {'k_k': 8.0,
     'gn_g': 2.846,
     'gn_b': 7.29,
     'q_norm_g': 6.982,
     'kv_norm_g': 8.0,
     'kidx_g': 7.654,
     'kidx_b': 8.0,
     'norm_g_l0_2': 8.0,
     'q_norm_g_l0_2': 8.0,
     'kv_norm_g_l0_2': 8.0,
     'mem_norm_g_l0_2': 8.0,
     'final_norm_g_2': 2.791}
    for name, (base, spread) in spreads.items():
        noise = np.random.default_rng([zlib.crc32(name.encode()), seed]).standard_normal(out[name].shape)
        drawn = base * np.exp(spread * noise) if base else spread * noise
        out[name] = __import__('jax').numpy.asarray(drawn.astype(out[name].dtype))
    for name, factor in factors.items():
        out[name] = (out[name] * factor).astype(out[name].dtype)
    return out
```

```python
import math
from contextlib import ExitStack

import numpy as np

import concourse.bass as bass
from concourse import mybir

F32 = mybir.dt.float32
BF16 = mybir.dt.bfloat16
I32 = mybir.dt.int32
ALU = mybir.AluOpType
ACT = mybir.ActivationFunctionType
AX = mybir.AxisListType.X

T = 2048
D = 1024
NT = T // 128
C = 64
UT = 256
NC = UT // C
TOPK = 256
NEG = -3.0e38
TAKEN = -3.3e38
BIAS = -1.0e30
DECAY = math.exp(-0.5)

K_ID, K_BLK, K_ONE, K_GM, K_LV, K_RS, K_SEL, K_NEG = 0, 128, 256, 384, 512, 1280, 1536, 1600
K_INV, K_PH, K_SGN, K_N = 1616, 1617, 1618, 1619

V_G1 = 0
V_MU = 8
V_MUL = 20
V_W0, V_A0, V_KK, V_KA, V_RK, V_GG, V_GB = 21, 25, 29, 33, 37, 41, 45
V_QN, V_KVN, V_IG, V_IB = 49, 51, 52, 53
V_G2, V_QN2, V_KVN2, V_GM = 54, 62, 65, 67
V_N = 75


class Queue:

    def __init__(self, sem):
        self.sem, self.n, self.ops, self.seen = sem, 0, [], {}

    def after(self, *toks):
        for t in toks:
            if t is None:
                continue
            if isinstance(t, list):
                self.after(*t)
                continue
            sem, v = t
            if self.seen.get(sem.name, 0) < v:
                self.seen[sem.name] = v
                self.ops.append((None, sem, v))

    def quiet(self, fn, *toks):
        self.after(*toks)
        self.ops.append((fn, None, 0))

    def __call__(self, fn, *toks):
        self.after(*toks)
        self.n += 1
        self.ops.append((fn, self.sem, 1))
        return (self.sem, self.n)

    def emit(self, e):
        for fn, sem, v in self.ops:
            if fn is None:
                e.wait_ge(sem, v)
            else:
                i = fn(e)
                if sem is not None:
                    i.then_inc(sem, v)


class Chan:

    def __init__(self, sem):
        self.sem, self.n = sem, 0

    def __call__(self, q, out, in_, *toks):
        q.after(*toks)
        if self.n:
            q.after((self.sem, self.n))
        self.n += 16
        q.ops.append((lambda e: e.dma_start(out, in_), self.sem, 16))
        return (self.sem, self.n)


class Bank:

    def __init__(self, t):
        self.t, self.free = t, []


class Buf:

    def __init__(self, t):
        self.t, self.ready, self.free = t, [], []


def merged(*gens):
    live = [[g, 0.0, w] for g, w in gens]
    while live:
        a = min(live, key=lambda x: x[1])
        try:
            next(a[0])
            a[1] += 1.0 / a[2]
        except StopIteration:
            live.remove(a)


def program(nc, A, upto=6):
    ctx = ExitStack()
    with ctx:
        def sem(n):
            return ctx.enter_context(nc.semaphore(n))

        pe, act, dve, pool, sp = (Queue(sem(n)) for n in ("s_pe", "s_act", "s_dve", "s_pool", "s_sp"))
        chans = {}

        def dma(name, q, out, in_, *toks):
            if name not in chans:
                chans[name] = Chan(sem("d_" + name))
            return chans[name](q, out, in_, *toks)

        def now():
            return [(q.sem, q.n) for q in (pe, act, dve, pool) if q.n] + [(c.sem, c.n) for c in chans.values()]

        def barrier():
            t = now()
            for q in (pe, act, dve, pool, sp):
                q.after(t)

        banks = [Bank(ctx.enter_context(nc.psum_tensor(f"ps{i}", [128, 512], F32))) for i in range(0)]
        big = ctx.enter_context(nc.psum_tensor("psum", [128, 4096], F32))
        banks = [Bank(big[:, 512 * i:512 * i + 512]) for i in range(8)]

        def mms(items, *toks):
            pe.after(*toks)
            t = None
            for n, it in enumerate(items):
                if len(it) == 3:
                    fn = lambda e, it=it: e.transpose(it[0], it[1], it[2])
                else:
                    fn = lambda e, it=it: e.matmul(it[0], it[1], it[2], start=it[3], stop=it[4],
                                                   skip_group_check=True)
                if n == len(items) - 1:
                    t = pe(fn)
                else:
                    pe.quiet(fn)
            return t

        def d_tt(o, a, b, op, *toks):
            return dve(lambda e: e.tensor_tensor(o, a, b, op), *toks)

        def d_ts(o, a, s1, s2, op0, op1, *toks):
            if op1 is None:
                return dve(lambda e: e.tensor_scalar(o, a, s1, None, op0), *toks)
            return dve(lambda e: e.tensor_scalar(o, a, s1, s2, op0, op1), *toks)

        def d_stt(o, a, s, b, op0, op1, *toks):
            return dve(lambda e: e.scalar_tensor_tensor(out=o, in0=a, scalar=s, in1=b, op0=op0, op1=op1), *toks)

        def d_copy(o, a, *toks):
            return dve(lambda e: e.tensor_copy(o, a), *toks)

        def p_tt(o, a, b, op, *toks):
            return pool(lambda e: e.tensor_tensor(o, a, b, op), *toks)

        def a_act(o, a, f, *toks, bias=0.0, scale=1.0, acc=None):
            if acc is None:
                return act(lambda e: e.activation(o, a, f, bias=bias, scale=scale), *toks)
            return act(lambda e: e.activation(o, a, f, bias=bias, scale=scale, accum_out=acc), *toks)

        def a_copy(o, a, *toks):
            return act(lambda e: e.activation(o, a, ACT.Copy), *toks)

        def rep(ap, n):
            return ap.unsqueeze(1).broadcast_to([ap.shape[0], n, ap.shape[1]])

        def spread(ap, n):
            return ap.unsqueeze(2).broadcast_to([ap.shape[0], ap.shape[1], n])

        scratch = {}
        for name, shape in (("xnT", [D, T]), ("cqT", [256, T]), ("thT", [64, T]), ("gaT", [512, T]), ("yT", [D, T]),
                            ("x1", [T, D]), ("gT", [D, T]), ("y2T", [D, T])):
            scratch[name] = A[name] if name in A else nc.dram_tensor("scr_" + name, shape, F32, kind="Internal").ap()

        def feat(name):
            return scratch[name].rearrange("(k p) t -> p k t", p=128)

        stored = []

        cst = ctx.enter_context(nc.sbuf_tensor("cst", [128, K_N], F32))
        vec = ctx.enter_context(nc.sbuf_tensor("vec", [128, V_N], F32))
        half = ctx.enter_context(nc.sbuf_tensor("half", [128, 16], F32))
        t_cst = dma("cst", sp, cst[:, :], A["cst"])
        t_vec = dma("vec", act, vec[:, :], A["vec"])
        ident = cst[:, K_ID:K_ID + 128]
        blk = cst[:, K_BLK:K_BLK + 128]
        one = cst[:, K_ONE:K_ONE + 128]
        neghalf = cst[:, K_NEG:K_NEG + 16]

        def v(i, n=1, p0=0, p1=128):
            return vec[p0:p1, i:i + n]

        class Stack:

            def __init__(self):
                self.c = ExitStack()

            def sb(self, name, shape, dt=F32):
                return self.c.enter_context(nc.sbuf_tensor(name, shape, dt))

            def close(self):
                self.c.close()
                barrier()

        def rsqrt(o, ss, ms, scale, eps, *toks):
            t = pool(lambda e: e.tensor_scalar(ms, ss, scale, eps, ALU.mult, ALU.add), *toks)
            return pool(lambda e: e.tensor_tensor(o, ms, neghalf[:, 0:o.shape[1]], ALU.pow), t, t_cst)

        def norm_in(st, name, source, dst, gain, keep=None):
            xin = [Buf(st.sb(f"{name}_x{i}", [128, D])) for i in range(3)]
            xn = [Buf(st.sb(f"{name}_n{i}", [128, D])) for i in range(2)]
            junk = st.sb(f"{name}_j", [128, D])
            ss = st.sb(f"{name}_ss", [128, 3 * NT])
            out = []
            tj = None
            for i in range(NT):
                b, n = xin[i % 3], xn[i % 2]
                t = dma(f"{name}{i % 3}", sp, b.t[:, :], source[128 * i:128 * i + 128, :], b.free)
                tj = a_act(junk[:, :], b.t[:, :], ACT.Square, t, tj, acc=ss[:, i:i + 1])
                t2 = rsqrt(ss[:, 2 * NT + i:2 * NT + i + 1], ss[:, i:i + 1], ss[:, NT + i:NT + i + 1],
                           1.0 / D, 1e-6, tj)
                t3 = d_ts(n.t[:, :], b.t[:, :], ss[:, 2 * NT + i:2 * NT + i + 1], None, ALU.mult, None, t, t2, n.free)
                b.free = [tj, t3]
                n.free = []
                for j in range(2):
                    k = banks[(2 * i + j) % 4]
                    t4 = mms([(k.t[:, 128 * q:128 * q + 128], n.t[:, 512 * j + 128 * q:512 * j + 128 * q + 128], ident)
                              for q in range(4)], t3, t_cst, k.free)
                    n.free = [t4]
                    t5 = d_tt(dst[:, 4 * j:4 * j + 4, 128 * i:128 * i + 128],
                              k.t.rearrange("p (a b) -> p a b", a=4),
                              spread(v(gain + 4 * j, 4), 128), ALU.mult, t4, t_vec)
                    k.free = [t5]
                    out.append(t5)
            return out

        P2 = Stack()
        ckvT = P2.sb("ckvT", [128, T])
        ckv = P2.sb("ckv", [128, NT, 128])
        kidx = P2.sb("kidx", [128, T])
        widx = P2.sb("widx", [128, NT, 4])
        w_uq = P2.sb("w_uq", [128, 2, 512])
        w_qi = P2.sb("w_qi", [128, 2, 256])
        w_uk = P2.sb("w_uk", [128, 8, 128])
        w_uv = P2.sb("w_uv", [128, 8, 64])
        t_wsm = [dma("w_uq", act, w_uq[:, :, :], A["w_uq"]), dma("w_qi", act, w_qi[:, :, :], A["w_qi"]),
                 dma("w_uk", act, w_uk[:, :, :], A["w_uk"]), dma("w_uv", act, w_uv[:, :, :], A["w_uv"])]

        def phase_a():
            st = Stack()
            xnT = st.sb("xnT", [128, 8, T])
            s1 = Stack()
            t_x = norm_in(s1, "xa", A["x"], xnT, V_G1)
            for k in range(8):
                stored.append(dma(f"xs{k}", sp, feat("xnT")[:, k, :], xnT[:, k, :], t_x))
            s1.close()
            wt = [Buf(st.sb(f"wt{i}", [128, 8, 128])) for i in range(3)]
            wl = st.sb("wl", [128, 8, 64])
            wx = st.sb("wx", [128, 8, 4])
            t_wl = dma("wl", act, wl[:, :, :], A["w_l"])
            t_wx = dma("wx", act, wx[:, :, :], A["w_x"])
            n = [0]
            nb = [0]

            def load(i):
                b = wt[n[0] % 3]
                b.ready = [dma(f"wt{n[0] % 3}", act, b.t[:, :, :], A["w_pre"][i], b.free)]
                n[0] += 1
                return b

            def bank():
                nb[0] += 1
                return banks[nb[0] % 8]

            def project(w, m, ch, *toks):
                k = bank()
                t = mms([(k.t[0:m, :], w[:, q, 0:m], xnT[:, q, 512 * ch:512 * ch + 512], q == 0, q == 7)
                         for q in range(8)], t_x, k.free, *toks)
                return k, t

            raw = [Buf(st.sb(f"raw{i}", [128, 2, 512])) for i in range(2)]
            sq = [Buf(st.sb(f"sq{i}", [128, 2, 512])) for i in range(2)]
            rs = [Buf(st.sb(f"rs{i}", [128, 512])) for i in range(2)]
            ot = [Buf(st.sb(f"ot{i}", [128, 2, 512])) for i in range(2)]
            lr = st.sb("lr", [64, T + 1])
            ld = st.sb("ld", [64, 512])
            th = st.sb("th", [64, T])
            eps = st.sb("eps", [128, 2])
            t_e = [pool(lambda e: e.memset(eps[:, 0:1], 1e-6)), pool(lambda e: e.memset(eps[:, 1:2], 1e-5))]

            t_l = [pool(lambda e: e.memset(lr[:, 0:1], 0.0))]
            for ch in range(4):
                k, t = project(wl, 64, ch, t_wl)
                t = a_copy(lr[:, 1 + 512 * ch:513 + 512 * ch], k.t[0:64, :], t)
                k.free = [t]
                t_l.append(t)
            td = None
            t_th = []
            for ch in range(4):
                p = lr[:, 1 + 512 * ch:513 + 512 * ch]
                td = d_tt(ld[:, :], lr[:, 512 * ch:512 + 512 * ch], p, ALU.subtract, t_l, td)
                td = d_stt(th[:, 512 * ch:512 * ch + 512], ld[:, :], v(V_MUL, 1, 0, 64), p, ALU.mult, ALU.add, td, t_vec)
                t_th += [a_act(th[0:32, 512 * ch:512 * ch + 512], th[0:32, 512 * ch:512 * ch + 512], ACT.Tanh, td)]
            stored.append(dma("th", sp, scratch["thT"], th[:, :], t_th, td))

            for what, tiles, ones, scale, e0 in (("q", 2, one, 1.0 / 256, 0), ("kv", 1, one, 1.0 / 128, 0),
                                                 ("ik", 1, blk, 1.0 / 64, 1)):
                ws = [load({"q": 0, "kv": 2, "ik": 3}[what] + j) for j in range(tiles)]
                for ch in range(4):
                    r, s, z, o = raw[ch % 2], sq[ch % 2], rs[ch % 2], ot[ch % 2]
                    tr = []
                    for j in range(tiles):
                        k, t = project(ws[j].t, 128, ch, ws[j].ready)
                        ws[j].free = [t]
                        tc = a_copy(r.t[:, j, :], k.t, t, r.free)
                        k.free = [tc]
                        tr.append(tc)
                    if what == "ik":
                        k = bank()
                        t = mms([(k.t, ones, r.t[:, 0, :], True, True)], tr, k.free)
                        t = d_stt(r.t[:, 0, :], k.t, -scale, r.t[:, 0, :], ALU.mult, ALU.add, t)
                        k.free = [t]
                        tr = [t]
                    ts = [a_act(s.t[:, j, :], r.t[:, j, :], ACT.Square, tr, s.free) for j in range(tiles)]
                    k = bank()
                    t = mms([(k.t, ones, s.t[:, j, :], j == 0, j == tiles - 1) for j in range(tiles)], ts, k.free)
                    s.free = [t]
                    t = a_act(z.t[:, :], k.t, ACT.Sqrt, t, t_e, z.free, bias=eps[:, e0:e0 + 1], scale=scale)
                    k.free = [t]
                    t = dve(lambda e, z=z: e.reciprocal(z.t[:, :], z.t[:, :]), t)
                    sl = slice(512 * ch, 512 * ch + 512)
                    if what == "q":
                        to = [d_stt(o.t[:, j, :], r.t[:, j, :], v(V_QN + j), z.t[:, :], ALU.mult, ALU.mult, t, o.free)
                              for j in range(2)]
                        o.free = [dma(f"cq{ch % 2}", sp, feat("cqT")[:, :, sl], o.t[:, :, :], to)]
                        stored.extend(o.free)
                    elif what == "kv":
                        to = [d_stt(ckvT[:, sl], r.t[:, 0, :], v(V_KVN), z.t[:, :], ALU.mult, ALU.mult, t)]
                        k = bank()
                        t = mms([(k.t[:, 128 * q:128 * q + 128],
                                  ckvT[:, 512 * ch + 128 * q:512 * ch + 128 * q + 128], ident) for q in range(4)], to, k.free)
                        k.free = [a_copy(ckv[:, 4 * ch:4 * ch + 4, :], k.t.rearrange("p (a b) -> p a b", a=4), t)]
                    else:
                        t = d_stt(o.t[:, 0, :], r.t[:, 0, :], v(V_IG), z.t[:, :], ALU.mult, ALU.mult, t, o.free)
                        to = [d_ts(kidx[:, sl], o.t[:, 0, :], v(V_IB), None, ALU.add, None, t)]
                        o.free = to
                    r.free = to
                    z.free = to
            k = bank()
            t = mms([(k.t[:, 4 * i:4 * i + 4], xnT[:, q, 128 * i:128 * i + 128], wx[:, q, :], q == 0, q == 7)
                     for i in range(NT) for q in range(8)], t_x, t_wx, k.free)
            k.free = [d_ts(widx[:, :, :], k.t[:, 0:64].rearrange("p (a b) -> p a b", a=NT), 0.5, None, ALU.mult, None, t)]
            for j in range(4):
                w = load(4 + j)
                for ch in range(4):
                    r, s, o = raw[ch % 2], sq[ch % 2], ot[ch % 2]
                    k, t = project(w.t, 128, ch, w.ready)
                    w.free = [t]
                    t1 = a_act(s.t[:, 0, :], k.t, ACT.Tanh, t, s.free, scale=0.5)
                    t2 = d_stt(o.t[:, 0, :], s.t[:, 0, :], 1.0, k.t, ALU.add, ALU.mult, t1, o.free)
                    k.free = [t2]
                    s.free = [t2]
                    o.free = [dma(f"ga{ch % 2}", sp, feat("gaT")[:, j, 512 * ch:512 * ch + 512], o.t[:, 0, :], t2)]
                    stored.extend(o.free)
            st.close()

        phase_a()

        def rwkv():
            sb = P2.sb
            wr = [Buf(sb(f"wr{i}", [128, 8, 128])) for i in range(4)]
            xs = Buf(sb("xs", [128, 8, UT]))
            tb = [Buf(sb(f"tb{i}", [64, UT])) for i in range(2)]
            pb = [Buf(sb(f"pb{i}", [128, 3, UT + 1])) for i in range(2)]
            vx = [Buf(sb(f"vx{i}", [128, C + UT])) for i in range(2)]
            lo = Buf(sb("lo", [64, 2, 128]))
            dd = sb("dd", [128, 3, UT])
            rk = sb("rk", [128, 2, UT])
            gr = sb("gr", [128, UT])
            tg_ = sb("tg_", [128, UT])
            sg = [Buf(sb(f"sg{i}", [128, UT])) for i in range(2)]
            bon = [Buf(sb(f"bon{i}", [128, UT])) for i in range(2)]
            tw = sb("tw", [128, 2, UT])
            lda = sb("lda", [128, 2, UT])
            LL = sb("LL", [128, 2, UT])
            PP = [Buf(sb(f"PP{i}", [128, 2, UT])) for i in range(2)]
            Pi = sb("Pi", [128, UT])
            kk0 = sb("kk0", [128, UT])
            inv = sb("inv", [128, UT])
            kkn = kk0
            k2 = sb("k2", [128, UT])
            b1 = kk0
            t1k = sb("t1k", [128, UT])
            AR = [Buf(sb(f"AR{i}", [128, NC, 2, C])) for i in range(2)]
            BK = sb("BK", [128, NC, 2, C])
            Gm = [Buf(sb(f"Gm{i}", [128, NC, 2, 2 * C])) for i in range(2)]
            BT = [Buf(sb(f"BT{i}", [128, NC, 128])) for i in range(2)]
            W = [Buf(sb(f"W{i}", [128, NC, 2, C])) for i in range(2)]
            Xu = [Buf(sb(f"Xu{i}", [128, NC, 128])) for i in range(2)]
            MV = [Buf(sb(f"MV{i}", [128, NC, C])) for i in range(2)]
            Xl = sb("Xl", [128, NC, 128])
            Lt = sb("Lt", [128, NC, 128])
            Lm = [Buf(sb("Lm", [128, NC, 128]))] * 2
            Y1 = sb("Y1", [128, NC, 128])
            Z = [Buf(sb(f"Z{i}", [128, C])) for i in range(2)]
            ZP = sb("ZP", [128, C])
            R = sb("R", [128, C])
            ys = sb("ys", [128, UT])
            yc = sb("yc", [128, UT])
            y2 = sb("y2", [128, UT])
            iv = y2
            yo = [Buf(sb(f"yo{i}", [128, UT])) for i in range(2)]
            epg = sb("epg", [128, 1])
            A_, B_, C_, S_, Y_ = banks[0:5]
            t_c = [t_cst, t_vec]
            t_h = dve(lambda e: e.tensor_scalar(half[:, 0:8], vec[:, V_W0:V_W0 + 8], 0.5, None, ALU.mult), t_c)
            t_k = dve(lambda e: e.tensor_scalar(half[:, 8:12], vec[:, V_KA:V_KA + 4], -1.0, 1.0, ALU.mult, ALU.add), t_c)
            t_ep = pool(lambda e: e.memset(epg[:, :], 64e-5))
            t_z = pool(lambda e: e.memset(Lt[:, :, :], 0.0))
            lvl = [cst[:, K_LV + 128 * i:K_LV + 128 * i + 128] for i in range(6)]
            gmask = cst[:, K_GM:K_GM + 128]
            S = {"xl": [], "y1": []}
            nw = [0]

            def wload(i):
                b = wr[nw[0] % 4]
                b.ready = [dma(f"wr{nw[0] % 4}", sp, b.t[:, :, :], A["w_rw"][i], b.free)]
                nw[0] += 1
                return b

            xsf = feat("xnT")
            st = {"free": {}}
            F = st["free"]

            def fr(*names):
                return [F[n] for n in names if n in F]

            wnow = {}

            def pre(u):
                hp, tg = divmod(u, T // UT)
                i2 = u % 2
                if tg == 0:
                    for j in range(4):
                        wnow[(hp, j)] = wload(4 * hp + j)
                    lo.ready = [dma("lo", sp, lo.t[:, :, :], A["w_lo"][:, :, 128 * hp:128 * hp + 128], lo.free)]
                x, tb_ = xs, tb[i2]
                t_th = dma(f"thl{i2}", sp, tb_.t[:, :], scratch["thT"][:, UT * tg:UT * tg + UT], tb_.free)
                tx = dma("xsl", sp, x.t[:, :, :], xsf[:, :, UT * tg:UT * tg + UT], x.free)
                p, q = pb[i2], pb[1 - i2]
                if tg == 0:
                    t_p0 = pool(lambda e: e.memset(p.t[:, :, 0:1], 0.0), p.free)
                else:
                    t_p0 = pool(lambda e: e.tensor_copy(p.t[:, :, 0:1], q.t[:, :, UT:UT + 1]), p.free, q.ready)
                sgb = sg[i2]
                tl = None
                toks = []
                for bk, pair in ((A_, (0, 1)), (B_, (2, 3))):
                    items = []
                    ws = [wnow[(hp, j)] for j in pair]
                    for n, w in enumerate(ws):
                        items += [(bk.t[:, UT * n:UT * n + UT], w.t[:, k, :], x.t[:, k, :], k == 0, k == 7)
                                  for k in range(8)]
                    t = mms(items[0:8], tx, bk.free, ws[0].ready, ws[1].ready)
                    yield
                    t = mms(items[8:16])
                    for w in ws:
                        w.free = [t]
                    x.free = [t]
                    if pair[0] == 0:
                        tl = a_copy(p.t[:, 0:2, 1:UT + 1], bk.t.rearrange("p (a b) -> p a b", a=2), t, p.free, t_p0)
                        bk.free = [tl]
                        toks.append(tl)
                    else:
                        t1 = a_copy(p.t[:, 2, 1:UT + 1], bk.t[:, 0:UT], t, p.free)
                        t2 = a_act(tg_[:, :], bk.t[:, UT:2 * UT], ACT.Tanh, t, fr("tg_"), scale=0.5)
                        t3 = a_copy(gr[:, :], bk.t[:, UT:2 * UT], t, fr("gr"))
                        bk.free = [t3]
                        toks.append(t1)
                    yield
                F["gr"] = F["tg_"] = d_stt(sgb.t[:, :], tg_[:, :], 1.0, gr[:, :], ALU.add, ALU.mult, t2, t3, sgb.free)
                sgb.ready = [F["gr"]]
                p.ready = toks + [t_p0]
                bk = C_
                t = mms([(bk.t[:, 0:UT], lo.t[:, 0, :], tb_.t[:, :], True, True),
                         (bk.t[:, UT:2 * UT], lo.t[:, 1, :], tb_.t[:, :], True, True)],
                        bk.free, lo.ready, t_th)
                tb_.free = lo.free = [t]
                t1 = a_act(tw[:, 0, :], bk.t[:, 0:UT], ACT.Tanh, t, fr("tw"), t_h, bias=half[:, hp:hp + 1], scale=0.5)
                t2 = a_act(tw[:, 1, :], bk.t[:, UT:2 * UT], ACT.Tanh, t, t_h, bias=half[:, 4 + hp:5 + hp], scale=0.5)
                bk.free = [t2]
                yield
                t = d_tt(dd[:, :, :], p.t[:, :, 0:UT], p.t[:, :, 1:UT + 1], ALU.subtract, p.ready, fr("dd"))
                V, Vq = vx[i2], vx[1 - i2]
                t_r = d_stt(rk[:, 0, :], dd[:, 0, :], v(V_MU + 3 * hp), p.t[:, 0, 1:UT + 1], ALU.mult, ALU.add, t, fr("rk0"))
                t_kx = d_stt(rk[:, 1, :], dd[:, 1, :], v(V_MU + 3 * hp + 1), p.t[:, 1, 1:UT + 1], ALU.mult, ALU.add, t, fr("rk1"))
                if tg == 0:
                    t_v0 = pool(lambda e: e.memset(V.t[:, 0:C], 0.0), V.free)
                else:
                    t_v0 = pool(lambda e: e.tensor_copy(V.t[:, 0:C], Vq.t[:, UT:UT + C]), V.free, Vq.ready)
                t_vv = d_stt(V.t[:, C:C + UT], dd[:, 2, :], v(V_MU + 3 * hp + 2), p.t[:, 2, 1:UT + 1], ALU.mult, ALU.add, t, V.free)
                V.ready = [t_vv, t_v0]
                F["dd"] = t_vv
                p.free = [t_vv]
                t_ld = d_ts(lda[:, 0, :], tw[:, 0, :], -0.5 * DECAY, -0.5 * DECAY, ALU.mult, ALU.add, t1, fr("lda0"))
                t_a = d_ts(lda[:, 1, :], tw[:, 1, :], 0.5, 0.5, ALU.mult, ALU.add, t2, fr("lda1"))
                F["tw"] = t_a
                t_L = dve(lambda e: e.tensor_tensor_scan(LL[:, 0, :], cst[:, K_RS:K_RS + UT], lda[:, 0, :], 0.0,
                                                         ALU.mult, ALU.add), t_ld, fr("LL"), t_c)
                t_Lp = d_tt(LL[:, 1, :], LL[:, 0, :], lda[:, 0, :], ALU.subtract, t_L)
                F["lda0"] = t_Lp
                pp = PP[i2]
                t_P = a_act(pp.t[:, :, :], LL[:, :, :], ACT.Exp, t_Lp, pp.free)
                t_Pi = a_act(Pi[:, :], LL[:, 0, :], ACT.Exp, t_L, fr("Pi"), scale=-1.0)
                F["LL"] = t_Pi
                yield
                t_k0 = d_ts(kk0[:, :], rk[:, 1, :], v(V_KK + hp), None, ALU.mult, None, t_kx, fr("kk0"))
                t = a_act(t1k[:, :], kk0[:, :], ACT.Square, t_k0, fr("t1k"))
                F["t1k"] = t = mms([(bk.t[:, 0:UT], blk, t1k[:, :], True, True)], t, bk.free)
                t = a_act(inv[:, :], bk.t[:, 0:UT], ACT.Sqrt, t, fr("inv"))
                bk.free = [t]
                t = d_ts(inv[:, :], inv[:, :], 1e-12, None, ALU.max, None, t)
                t_i = dve(lambda e: e.reciprocal(inv[:, :], inv[:, :]), t)
                yield
                t_kn = d_tt(kkn[:, :], kk0[:, :], inv[:, :], ALU.mult, t_i)
                F["inv"] = t_kn
                t_u = d_ts(t1k[:, :], lda[:, 1, :], v(V_KA + hp), half[:, 8 + hp:9 + hp], ALU.mult, ALU.add, t_a, t_k, fr("t1k"))
                t_k2 = d_tt(k2[:, :], rk[:, 1, :], t1k[:, :], ALU.mult, t_u, fr("k2"))
                F["t1k"] = F["rk1"] = t_k2
                a_ = AR[i2]

                def ch(ap):
                    return ap.rearrange("p (c t) -> p c t", c=NC)

                t_al = d_stt(a_.t[:, :, 0, :], ch(pp.t[:, 1, :]), -1.0, ch(kkn[:, :]), ALU.mult, ALU.mult, t_P, t_kn, a_.free)
                t_rh = p_tt(a_.t[:, :, 1, :], ch(pp.t[:, 0, :]), ch(rk[:, 0, :]), ALU.mult, t_P, t_r, a_.free)
                a_.ready = [t_al, t_rh]
                t_b = d_tt(b1[:, :], kkn[:, :], lda[:, 1, :], ALU.mult, t_kn, t_al)
                F["lda1"] = t_b
                t_bq = d_stt(t1k[:, :], rk[:, 0, :], v(V_RK + hp), k2[:, :], ALU.mult, ALU.mult, t_k2, fr("t1k"))
                F["rk0"] = [t_bq, t_rh]
                t1 = d_tt(BK[0:64, :, 0, :], ch(b1[0:64, :]), ch(Pi[0:64, :]), ALU.mult, t_b, t_Pi, fr("BK"))
                t2 = d_tt(BK[64:128, :, 1, :], ch(b1[64:128, :]), ch(Pi[64:128, :]), ALU.mult)
                t3 = d_tt(BK[0:64, :, 1, :], ch(k2[0:64, :]), ch(Pi[0:64, :]), ALU.mult)
                t4 = d_tt(BK[64:128, :, 0, :], ch(k2[64:128, :]), ch(Pi[64:128, :]), ALU.mult)
                F["kk0"], F["Pi"], F["k2"] = t2, t4, t4
                t_BK = t4
                yield
                F["t1k"] = t = mms([(bk.t[:, 0:UT], blk, t1k[:, :], True, True)], t_bq, bk.free)
                bn = bon[i2]
                bn.ready = [d_tt(bn.t[:, :], bk.t[:, 0:UT], V.t[:, C:C + UT], ALU.mult, t, t_vv, bn.free)]
                bk.free = bn.ready
                g = Gm[i2]
                tg2 = []
                for e in range(2):
                    kb = (A_, B_)[e]
                    t = mms([(kb.t[:, 128 * c:128 * c + 128], BK[64 * e:64 * e + 64, c, :, :],
                              a_.t[64 * e:64 * e + 64, c, :, :], True, True) for c in range(NC)],
                            t_BK, a_.ready, kb.free)
                    t = d_tt(g.t[:, :, e, :], kb.t.rearrange("p (a b) -> p a b", a=4), rep(gmask, 4), ALU.mult, t, g.free)
                    kb.free = [t]
                    tg2.append(t)
                    yield
                g.ready = tg2
                t_lt = [a_copy(Lt[0:64, :, 0:64], g.t[0:64, :, 0, 0:64], tg2, t_z, fr("Lt")),
                        a_copy(Lt[64:128, :, 64:128], g.t[64:128, :, 1, 0:64])]
                bt = BT[i2]
                t = mms([(A_.t[:, 128 * c:128 * c + 128], BK[:, c, :, :], ident) for c in range(NC)], A_.free)
                F["BK"] = t
                bt.ready = [a_copy(bt.t[:, :, :], A_.t.rearrange("p (c t) -> p c t", c=NC), t, bt.free)]
                A_.free = bt.ready
                w = W[i2]
                t = mms([(B_.t[:, 128 * c:128 * c + 128], V.t[:, C * c:C * c + 128], ident) for c in range(NC)],
                        B_.free, V.ready)
                t5 = mms([(C_.t[0:64, 0:128], V.t[:, UT:UT + C], ident)], C_.free)
                V.free = [t5, bn.ready]
                bv = B_.t.rearrange("p (c e i) -> p c e i", c=NC, e=2)
                t1 = a_copy(w.t[64:128, :, 0, :], bv[64:128, :, 0, :], t, w.free)
                t2 = a_copy(w.t[0:64, 0:NC - 1, 1, :], bv[0:64, 1:NC, 1, :])
                B_.free = [t2]
                t3 = a_copy(w.t[0:64, NC - 1, 1, :], C_.t[0:64, 64:128], t5)
                C_.free = [t3]
                w.ready = [t1, t2, t3]
                yield
                mv = MV[i2]
                t = mms([(C_.t[64 * e:64 * e + 64, C * c:C * c + C], g.t[64 - 64 * e:128 - 64 * e, c, e, 0:64],
                          w.t[64 - 64 * e:128 - 64 * e, c, e, :], True, True) for e in range(2) for c in range(NC)],
                        w.ready, g.ready, C_.free)
                mv.ready = [a_copy(mv.t[:, :, :], C_.t[:, 0:UT].rearrange("p (c t) -> p c t", c=NC), t, mv.free)]
                C_.free = mv.ready
                xu = Xu[i2]
                t_m = p_tt(Lm[0].t[:, :, :], Lt[:, :, :], rep(lvl[0], NC), ALU.mult, t_lt, Lm[0].free, t_c)
                t_u = d_tt(xu.t[:, :, :], Lm[0].t[:, :, :], rep(ident, NC), ALU.add, t_m, xu.free)
                Lm[0].free = [t_u]
                t = mms([(A_.t[:, 128 * c:128 * c + 128], xu.t[:, c, :], ident) for c in range(NC)], t_u, A_.free)
                t_l = a_copy(Xl[:, :, :], A_.t.rearrange("p (c t) -> p c t", c=NC), t, fr("Xl"))
                A_.free = [t_l]
                for lv in range(1, 6):
                    m = Lm[lv % 2]
                    t_m = p_tt(m.t[:, :, :], Lt[:, :, :], rep(lvl[lv], NC), ALU.mult, m.free)
                    yield
                    t = mms([(A_.t[:, 128 * c:128 * c + 128], m.t[:, c, :], Xl[:, c, :], True, True) for c in range(NC)],
                            t_m, t_l, A_.free)
                    m.free = [t]
                    t_y = a_copy(Y1[:, :, :], A_.t.rearrange("p (c t) -> p c t", c=NC), t, fr("Y1"))
                    A_.free = [t_y]
                    yield
                    if lv < 5:
                        t = mms([(B_.t[:, 128 * c:128 * c + 128], xu.t[:, c, :], Y1[:, c, :], True, True)
                                 for c in range(NC)], t_y, t_u, B_.free)
                        t_l2 = d_tt(Xl[:, :, :], Xl[:, :, :], B_.t.rearrange("p (c t) -> p c t", c=NC), ALU.add, t)
                        B_.free = [t_l2]
                    t = mms([(A_.t[:, 128 * c:128 * c + 128], Y1[:, c, :], xu.t[:, c, :], True, True)
                             for c in range(NC)], t_y, t_u, A_.free)
                    F["Y1"] = t
                    t_u = d_tt(xu.t[:, :, :], xu.t[:, :, :], A_.t.rearrange("p (c t) -> p c t", c=NC), ALU.add, t)
                    A_.free = [t_u]
                    if lv < 5:
                        t_l = t_l2
                    else:
                        F["Xl"] = t_u
                F["Lt"] = t_m
                xu.ready = [t_u]
                yield

            nz = [0]

            def seq(u):
                hp, tg = divmod(u, T // UT)
                i2 = u % 2
                a_, g, bt, w, xu, pp, mv = AR[i2], Gm[i2], BT[i2], W[i2], Xu[i2], PP[i2], MV[i2]
                z = Z[nz[0] % 2]
                if tg == 0:
                    z.ready = [pool(lambda e, z=z: e.memset(z.t[:, :], 0.0), z.free, z.ready)]
                ty = []
                for c in range(NC):
                    z, zn = Z[nz[0] % 2], Z[(nz[0] + 1) % 2]
                    items = []
                    for e in range(2):
                        a = 64 * e
                        items.append((S_.t[a:a + 64, 0:64], a_.t[a:a + 64, c, 0, :], z.t[a:a + 64, :], True, True))
                    t = mms(items, z.ready, a_.ready, g.ready, w.ready, S_.free)
                    t_zp = dve(lambda e, z=z, c=c: e.tensor_scalar(ZP[:, :], z.t[:, :], pp.t[:, 0, C * c + C - 1:C * c + C], None,
                                                                   ALU.mult), z.ready, fr("ZP"))
                    t_R = d_tt(R[:, :], S_.t[:, 0:64], mv.t[:, c, :], ALU.add, t, mv.ready, fr("R"))
                    yield
                    t = mms([(S_.t[:, 64:128], xu.t[:, c, :], R[:, :], True, True)], t_R, xu.ready)
                    F["R"] = t
                    t1 = d_copy(w.t[0:64, c, 0, :], S_.t[0:64, 64:128], t)
                    t2 = d_copy(w.t[64:128, c, 1, :], S_.t[64:128, 64:128])
                    yield
                    t = mms([(S_.t[64 * e:64 * e + 64, 128:192], bt.t[:, c, 64 * e:64 * e + 64], w.t[:, c, e, :], True, True)
                             for e in range(2)], t1, t2, bt.ready)
                    t_z = d_stt(zn.t[:, :], S_.t[:, 128:192], pp.t[:, 0, C * c + C - 1:C * c + C], ZP[:, :],
                                ALU.mult, ALU.add, t, t_zp, zn.free)
                    zn.ready = [t_z]
                    F["ZP"] = t_z
                    S_.free = [t_z]
                    items = []
                    for e in range(2):
                        a = 64 * e
                        o = Y_.t[a:a + 64, C * c:C * c + C]
                        items.append((o, z.t[a:a + 64, :], a_.t[a:a + 64, c, 1, :], True, False))
                        items.append((o, w.t[:, c, e, :], g.t[:, c, e, C:2 * C], False, True))
                    ty = mms(items, Y_.free if c == 0 else None)
                    z.free = [ty, t_zp]
                    nz[0] += 1
                    yield
                a_.free = g.free = bt.free = w.free = xu.free = [ty]
                mv.free = [t_R]
                pp.free = [t_z, ty] + a_.ready
                t = a_copy(ys[:, :], Y_.t[:, 0:UT], ty, fr("ys"))
                Y_.free = [t]
                t = mms([(S_.t[:, 256:512], blk, ys[:, :], True, True)], t, S_.free)
                t = d_stt(yc[:, :], S_.t[:, 256:512], -1.0 / 64, ys[:, :], ALU.mult, ALU.add, t, fr("yc"))
                F["ys"] = S_.free = t
                t = a_act(y2[:, :], yc[:, :], ACT.Square, t, fr("y2"))
                yield
                t = mms([(S_.t[:, 256:512], blk, y2[:, :], True, True)], t, S_.free)
                t = a_act(iv[:, :], S_.t[:, 256:512], ACT.Sqrt, t, t_ep, bias=epg[:, :], scale=1.0 / 64)
                S_.free = [t]
                t = dve(lambda e: e.reciprocal(iv[:, :], iv[:, :]), t)
                t = d_tt(yc[:, :], yc[:, :], iv[:, :], ALU.mult, t)
                F["y2"] = t
                t = d_ts(yc[:, :], yc[:, :], v(V_GG + hp), v(V_GB + hp), ALU.mult, ALU.add, t)
                bn, s, o = bon[i2], sg[i2], yo[i2]
                t = d_tt(yc[:, :], yc[:, :], bn.t[:, :], ALU.add, t, bn.ready)
                t = d_stt(o.t[:, :], yc[:, :], 0.5, s.t[:, :], ALU.mult, ALU.mult, t, s.ready, o.free)
                F["yc"] = t
                bn.free = s.free = [t]
                o.free = [dma(f"yo{i2}", sp, feat("yT")[:, hp, UT * tg:UT * tg + UT], o.t[:, :], t)]
                stored.extend(o.free)
                yield

            def both(g1, g2):
                live = [g for g in (g1, g2) if g is not None]
                while live:
                    for g in list(live):
                        try:
                            next(g)
                            yield
                        except StopIteration:
                            live.remove(g)

            NU = 4 * (T // UT)
            for u in range(NU + 1):
                yield from both(pre(u) if u < NU else None, seq(u - 1) if u else None)

        def dsa():
            sb = P2.sb
            cq = [Buf(sb(f"cq{i}", [128, 2, 128])) for i in range(2)]
            gate = [Buf(sb(f"gt{i}", [128, 4, 128])) for i in range(1)]
            qT = sb("qT", [128, 4, 128])
            qa = [Buf(sb(f"qa{i}", [128, 8, 128])) for i in range(2)]
            qi = sb("qi", [128, 2, 128])
            rl = [Buf(sb(f"rl{i}", [128, 512])) for i in range(2)]
            score = Buf(sb("score", [128, T]))
            bias = [Buf(sb(f"bias{i}", [128, T], BF16)) for i in range(2)]
            m8 = sb("m8", [128, 8])
            Pb = [Buf(sb(f"P{i}", [128, T])) for i in range(2)]
            pt = [Buf(sb(f"pt{i}", [128, 512])) for i in range(2)]
            mx = [Buf(sb(f"mx{i}", [128, 8])) for i in range(2)]
            sm = sb("sm", [128, 16])
            ol = sb("ol", [128, 4, 128])
            oT = sb("oT", [128, 4, 128])
            yo = [Buf(sb(f"ya{i}", [128, 4, 128])) for i in range(1)]
            D0, D1, D2 = banks[5:8]
            F = {}

            def fr(*names):
                return [F[n] for n in names if n in F]

            nd = [0]
            nx = [0]

            def dbank():
                nd[0] += 1
                return (D0, D1)[nd[0] % 2]

            def index(b):
                N = 128 * (b + 1)
                c = cq[b % 2]
                tq = dma(f"cql{b % 2}", sp, c.t[:, :, :], feat("cqT")[:, :, 128 * b:128 * b + 128], c.free)
                k = dbank()
                t = mms([(k.t[:, 128 * m:128 * m + 128], w_uq[:, j, 128 * m:128 * m + 128], c.t[:, j, :], j == 0, j == 1)
                         for m in range(4) for j in range(2)], tq, t_wsm, k.free)
                t_q = a_copy(qT[:, :, :], k.t.rearrange("p (a b) -> p a b", a=4), t, fr("qT"))
                k.free = [t_q]
                k = dbank()
                t = mms([(k.t[:, 128 * m:128 * m + 128], w_qi[:, j, 128 * m:128 * m + 128], c.t[:, j, :], j == 0, j == 1)
                         for m in range(2) for j in range(2)], tq, k.free)
                c.free = [t]
                t_i = a_copy(qi[:, :, :], k.t[:, 0:256].rearrange("p (a b) -> p a b", a=2), t, fr("qi"))
                k.free = [t_i]
                yield
                q = qa[b % 2]
                q.ready = []
                for h in range(2):
                    k = dbank()
                    t = mms([(k.t[:, 128 * m:128 * m + 128],
                              w_uk[:, 4 * h + m, :], qT[:, 2 * h + m // 2, :], True, True) for m in range(4)],
                            t_q, k.free)
                    F["qT"] = t
                    t = a_act(q.t[:, 4 * h:4 * h + 4, :], k.t.rearrange("p (a b) -> p a b", a=4), ACT.Copy, t, q.free,
                              scale=0.125)
                    k.free = [t]
                    q.ready.append(t)
                bi = bias[b % 2]
                if b < TOPK // 128:
                    t = pool(lambda e: e.memset(bi.t[:, 0:N], 0.0), bi.free)
                    bi.ready = [pool(lambda e: e.affine_select(out=bi.t[:, 128 * b:N], in_=bi.t[:, 128 * b:N],
                                                               compare_op=ALU.is_ge, fill=BIAS, base=0,
                                                               pattern=[[-1, 128]], channel_multiplier=1), t)]
                    yield
                    return
                last = []
                for s0 in range(0, N, 512):
                    w = min(512, N - s0)
                    sc = score.t[:, s0:s0 + w]
                    ts = None
                    for h in range(4):
                        k = dbank()
                        a = 64 * (h % 2)
                        t = mms([(k.t[:, 0:w], qi[a:a + 64, h // 2, :], kidx[a:a + 64, s0:s0 + w], True, True)], t_i, k.free)
                        r = rl[h % 2]
                        t = a_act(r.t[:, 0:w], k.t[:, 0:w], ACT.Relu, t, r.free)
                        k.free = [t]
                        wi = widx[:, b, h:h + 1]
                        if h == 0:
                            ts = d_ts(sc, r.t[:, 0:w], wi, None, ALU.mult, None, t, score.free)
                        else:
                            ts = d_stt(sc, r.t[:, 0:w], wi, sc, ALU.mult, ALU.add, t, ts)
                        r.free = [ts]
                    last.append(ts)
                    yield
                F["qi"] = (pe.sem, pe.n)
                t = pool(lambda e: e.affine_select(out=score.t[:, 128 * b:N], in_=score.t[:, 128 * b:N],
                                                   compare_op=ALU.is_ge, fill=NEG, base=0,
                                                   pattern=[[-1, 128]], channel_multiplier=1), last)
                s = score.t[:, 0:N]
                for r in range(TOPK // 8):
                    t = dve(lambda e: e.max(m8[:, :], s), t)
                    t = dve(lambda e: e.match_replace(out=s, in_to_replace=m8[:, :], in_values=s, imm_value=TAKEN), t)
                    yield
                t = d_ts(bi.t[:, 0:N], s, TAKEN, BIAS, ALU.not_equal, ALU.mult, t, bi.free)
                bi.ready = [t]
                score.free = [t]

            def attend(b):
                N = 128 * (b + 1)
                q, bi = qa[b % 2], bias[b % 2]
                g = gate[0]
                tg = dma("gal", sp, g.t[:, :, :], feat("gaT")[:, :, 128 * b:128 * b + 128], g.free)
                chunks = [(s0, min(512, N - s0)) for s0 in range(0, N, 512)]
                kf = dbank
                t_oT = []
                t_pend = None

                def scores(h):
                    p, m = Pb[h % 2], mx[h % 2]
                    tt = []
                    for n, (s0, w) in enumerate(chunks):
                        k = kf()
                        t = mms([(k.t[:, 0:w], q.t[:, h, :], ckvT[:, s0:s0 + w], True, True)], q.ready, k.free)
                        t = dve(lambda e, p=p, m=m, n=n, s0=s0, w=w, k=k: e.tensor_tensor_reduce(
                            p.t[:, s0:s0 + w], k.t[:, 0:w], bi.t[:, s0:s0 + w], 1.0, -3.0e38, ALU.add, ALU.max,
                            m.t[:, n:n + 1]), t, bi.ready, p.free, m.free)
                        k.free = [t]
                        tt.append(t)
                    t = dve(lambda e: e.tensor_reduce(m.t[:, 4:5], m.t[:, 0:len(chunks)], AX, ALU.max, negate=True), tt)
                    t = a_act(p.t[:, 0:N], p.t[:, 0:N], ACT.Exp, t, tt, fr("sm"), bias=m.t[:, 4:5], acc=sm[:, h:h + 1])
                    m.free = [t]
                    p.ready = [t]

                def values(h):
                    p = Pb[h % 2]
                    np_ = [0]
                    td = None
                    first = True
                    for s0, w in chunks:
                        k = kf()
                        n = w // 128
                        t = mms([(k.t[:, 128 * j:128 * j + 128], p.t[:, s0 + 128 * j:s0 + 128 * j + 128], ident)
                                 for j in range(n)], p.ready, k.free)
                        x = pt[nx[0] % 2]
                        nx[0] += 1
                        if (s0 // 512) % 2:
                            t = d_copy(x.t[:, 0:w], k.t[:, 0:w], t, x.free)
                        else:
                            t = a_copy(x.t[:, 0:w], k.t[:, 0:w], t, x.free)
                        k.free = [t]
                        hh = h % 4
                        td = mms([(D2.t[:, 128 * hh:128 * hh + 128], x.t[:, 128 * j:128 * j + 128],
                                   ckv[:, s0 // 128 + j, :], s0 + j == 0, s0 + w == N and j == n - 1)
                                  for j in range(n)], t, D2.free if (hh == 0 and s0 == 0) else None)
                        x.free = [td]
                    p.free = [td]
                    return td

                def finish(h4, td):
                    t = dve(lambda e: e.reciprocal(sm[:, 8 + 4 * h4:12 + 4 * h4], sm[:, 4 * h4:4 * h4 + 4]), Pb[0].ready, Pb[1].ready)
                    t = d_tt(ol[:, :, :], D2.t.rearrange("p (a b) -> p a b", a=4),
                             spread(sm[:, 8 + 4 * h4:12 + 4 * h4], 128), ALU.mult, td, t, fr("ol"))
                    D2.free = [t]
                    k = kf()
                    t = mms([(k.t[:, 128 * j:128 * j + 128], ol[:, j, :], ident) for j in range(4)], t, k.free)
                    F["ol"] = t
                    t = a_copy(oT[:, :, :], k.t.rearrange("p (a b) -> p a b", a=4), t, fr("oT"))
                    k.free = [t]
                    k = kf()
                    F["oT"] = t = mms([(k.t[64 * (h % 2):64 * (h % 2) + 64, 128 * (h // 2):128 * (h // 2) + 128],
                                        w_uv[:, 4 * h4 + h, :], oT[:, h, :], True, True) for h in range(4)], t, k.free)
                    y = yo[0]
                    t = d_stt(y.t[:, 2 * h4:2 * h4 + 2, :], k.t[:, 0:256].rearrange("p (a b) -> p a b", a=2), 0.5,
                              g.t[:, 2 * h4:2 * h4 + 2, :], ALU.mult, ALU.mult, t, tg, y.free)
                    k.free = [t]
                    if h4 == 1:
                        F["sm"] = g.free = t
                        y.free = [dma("ya", sp, feat("yT")[:, 4:8, 128 * b:128 * b + 128], y.t[:, :, :], t)]
                        stored.extend(y.free)

                scores(0)
                yield
                for h in range(8):
                    if h < 7:
                        scores(h + 1)
                        yield
                    td = values(h)
                    if h % 4 == 3:
                        finish(h // 4, td)
                    yield
                q.free = bi.free = [(pe.sem, pe.n), (dve.sem, dve.n)]
                yield

            yield from index(0)
            for b in range(NT):
                gi = index(b + 1) if b + 1 < NT else None
                ga = attend(b)
                live = [g for g in (gi, ga) if g]
                while live:
                    for g in list(live):
                        try:
                            next(g)
                            if g is gi:
                                next(g)
                            yield
                        except StopIteration:
                            live.remove(g)

        if upto >= 2:
            merged((rwkv(), 1.0), (dsa(), 0.6))
        P2.close()

        def mix_out(st, sb, name, source, w_src, resid, gsrc, tile_done):
            w = st.sb(f"{name}_w", [128, 8, D])
            gf = sb(f"{name}_g", [128, D])
            t_w = [dma(f"{name}w{k}", act, w[:, k, :], w_src[k]) for k in range(8)]
            t_g = dma(f"{name}g", act, gf[:, :], gsrc)
            yt = [Buf(sb(f"{name}_y{i}", [128, 8, 128])) for i in range(2)]
            xr = [Buf(sb(f"{name}_r{i}", [128, D])) for i in range(2)]
            xo = [Buf(sb(f"{name}_o{i}", [128, D])) for i in range(2)]
            xg = [Buf(sb(f"{name}_q{i}", [128, D])) for i in range(2)]
            junk = sb(f"{name}_j", [128, D])
            ss = sb(f"{name}_ss", [128, 3 * NT])
            tj = [None]
            for i in range(NT):
                y, x, o, g = yt[i % 2], xr[i % 2], xo[i % 2], xg[i % 2]
                ty = dma(f"{name}y{i % 2}", sp, y.t[:, :, :], feat(source)[:, :, 128 * i:128 * i + 128], y.free)
                tx = dma(f"{name}r{i % 2}", act, x.t[:, :], resid[128 * i:128 * i + 128, :], x.free)
                to = []
                for n in range(2):
                    k = banks[2 * (i % 2) + n]
                    t = mms([(k.t, y.t[:, q, :], w[:, q, 512 * n:512 * n + 512], q == 0, q == 7) for q in range(8)],
                            ty, t_w, k.free)
                    y.free = [t]
                    t = d_tt(o.t[:, 512 * n:512 * n + 512], k.t, x.t[:, 512 * n:512 * n + 512], ALU.add, t, tx, o.free)
                    k.free = [t]
                    to.append(t)
                x.free = to
                tj[0] = a_act(junk[:, :], o.t[:, :], ACT.Square, to, tj[0], acc=ss[:, i:i + 1])
                t2 = rsqrt(ss[:, 2 * NT + i:2 * NT + i + 1], ss[:, i:i + 1], ss[:, NT + i:NT + i + 1], 1.0 / D, 1e-6, tj[0])
                t3 = d_stt(g.t[:, :], o.t[:, :], ss[:, 2 * NT + i:2 * NT + i + 1], gf[:, :], ALU.mult, ALU.mult,
                           t2, t_g, g.free)
                o.free = [t3, tj[0]]
                tile_done(i, g, t3)
            return

        def phase3(sb=None):
            P4 = Stack()
            hT = P4.sb("hT", [128, 8, T])
            st = Stack()
            sb = sb or st.sb
            hn = [Buf(sb(f"hn{i}", [128, D])) for i in range(2)]
            ss = st.sb("h_ss", [128, 3 * NT])
            junk = sb("h_j", [128, D])
            tj = [None]
            t_h = []

            def done(i, g, t):
                ts = dma(f"x1{i % 2}", sp, scratch["x1"][128 * i:128 * i + 128, :], g.t[:, :], t)
                stored.append(ts)
                tj[0] = a_act(junk[:, :], g.t[:, :], ACT.Square, t, tj[0], acc=ss[:, i:i + 1])
                t2 = rsqrt(ss[:, 2 * NT + i:2 * NT + i + 1], ss[:, i:i + 1], ss[:, NT + i:NT + i + 1], 1.0 / D, 1e-6, tj[0])
                n = hn[i % 2]
                t3 = d_ts(n.t[:, :], g.t[:, :], ss[:, 2 * NT + i:2 * NT + i + 1], None, ALU.mult, None, t2, n.free)
                g.free = [ts, tj[0], t3]
                for j in range(2):
                    k = banks[4 + (2 * i + j) % 4]
                    t4 = mms([(k.t[:, 128 * q:128 * q + 128], n.t[:, 512 * j + 128 * q:512 * j + 128 * q + 128], ident)
                              for q in range(4)], t3, k.free)
                    n.free = [t4]
                    t5 = d_tt(hT[:, 4 * j:4 * j + 4, 128 * i:128 * i + 128], k.t.rearrange("p (a b) -> p a b", a=4),
                              spread(v(V_G2 + 4 * j, 4), 128), ALU.mult, t4)
                    k.free = [t5]
                    t_h.append(t5)

            mix_out(st, sb, "m1", "yT", A["w_out"], A["x"], A["final_g"], done)
            st.close()
            return P4, hT, t_h

        def phase45():
            P5 = Stack()
            sb5 = P5.sb
            cqT = sb5("cq2", [128, 3, T])
            ckv2 = sb5("ckv2", [128, 2, T])
            KB = [Buf(sb5(f"KB{i}", [128, T])) for i in range(2)]
            kmT = sb5("kmT", [128, 2, 256])
            vm = sb5("vm", [128, 2, 256])
            qm = sb5("qm", [128, 2, T])
            CS = sb5("CS", [128, T])
            spare = [cqT.rearrange("p a t -> p (a t)"), ckv2.rearrange("p a t -> p (a t)"), qm.rearrange("p a t -> p (a t)"),
                     KB[0].t, KB[1].t, CS]
            spare = [[x[:, :], 0] for x in spare]

            def carve(name, shape):
                n = shape[1] * (shape[2] if len(shape) > 2 else 1)
                x = next(x for x in spare if x[0].shape[1] - x[1] >= n)
                ap = x[0][:, x[1]:x[1] + n]
                x[1] += n
                return ap.rearrange("p (a b) -> p a b", a=shape[1]) if len(shape) > 2 else ap

            P4, hT, t_h = phase3(carve)
            st = Stack()
            wt = [Buf(st.sb(f"w4{i}", [128, 8, 128])) for i in range(3)]
            raw = [Buf(st.sb(f"raw4{i}", [128, 3, 512])) for i in range(2)]
            z2 = [Buf(st.sb(f"z4{i}", [128, 512])) for i in range(2)]
            eps = st.sb("eps4", [128, 1])
            t_e = pool(lambda e: e.memset(eps[:, :], 1e-6))
            n = [0]
            nb = [0]

            def load(i):
                b = wt[n[0] % 3]
                b.ready = [dma(f"w4{n[0] % 3}", act, b.t[:, :, :], A["w_in2"][i], b.free)]
                n[0] += 1
                return b

            def bank():
                nb[0] += 1
                return banks[nb[0] % 8]

            s2 = Stack()
            posi = s2.sb("posi", [128, T], I32)
            an = s2.sb("an", [128, T])
            kr = s2.sb("kr", [128, T])
            t = dma("pos", sp, posi[64:128, :], A["pos"])
            t = d_copy(an[64:128, :], posi[64:128, :], t)
            t = d_ts(an[64:128, :], an[64:128, :], cst[64:128, K_INV:K_INV + 1], None, ALU.mult, None, t)
            t = d_ts(kr[64:128, :], an[64:128, :], 1.0 / (2 * math.pi), cst[64:128, K_PH:K_PH + 1], ALU.mult, ALU.add, t)
            t = d_ts(kr[64:128, :], kr[64:128, :], 12582912.0, -12582912.0, ALU.add, ALU.add, t)
            c1 = 6.28125
            c2 = float(np.float32(2 * math.pi - c1))
            t = d_stt(an[64:128, :], kr[64:128, :], -c1, an[64:128, :], ALU.mult, ALU.add, t)
            t = d_stt(an[64:128, :], kr[64:128, :], -c2, an[64:128, :], ALU.mult, ALU.add, t)
            t = d_ts(kr[64:128, :], cst[64:128, K_PH:K_PH + 1].broadcast_to([64, T]), 2 * math.pi, None, ALU.mult, None, t)
            t = d_tt(an[64:128, :], an[64:128, :], kr[64:128, :], ALU.add, t)
            t = d_ts(an[64:128, :], an[64:128, :], 3.1415925, -3.1415925, ALU.min, ALU.max, t)
            t = a_act(CS[64:128, :], an[64:128, :], ACT.Sin, t)
            t_cs = [d_ts(CS[64:128, :], CS[64:128, :], cst[64:128, K_SGN:K_SGN + 1], None, ALU.mult, None, t),
                    pool(lambda e: e.memset(CS[0:64, :], 1.0))]
            s2.close()
            sq = [Buf(st.sb(f"sq4{i}", [128, 3, 512])) for i in range(2)]
            ot = [Buf(st.sb(f"o4{i}", [128, 512])) for i in range(2)]
            th2 = [Buf(st.sb(f"t4{i}", [128, 512])) for i in range(2)]

            def project(w, m0, m1, ch, *toks):
                k = bank()
                t = mms([(k.t[m0:m1, :], w[:, q, 0:m1 - m0], hT[:, q, 512 * ch:512 * ch + 512], q == 0, q == 7)
                         for q in range(8)], t_h, k.free, *toks)
                return k, t

            ready = {}
            for dst, base, tiles, vg in ((cqT, 0, 3, V_QN2), (ckv2, 3, 2, V_KVN2)):
                ws = [load(base + j) for j in range(tiles)]
                for ch in range(4):
                    r, s, z = raw[ch % 2], sq[ch % 2], z2[ch % 2]
                    tr = []
                    for j in range(tiles):
                        k, t = project(ws[j].t, 0, 128, ch, ws[j].ready)
                        ws[j].free = [t]
                        t = a_copy(r.t[:, j, :], k.t, t, r.free)
                        k.free = [t]
                        tr.append(t)
                    ts = [a_act(s.t[:, j, :], r.t[:, j, :], ACT.Square, tr, s.free) for j in range(tiles)]
                    k = bank()
                    t = mms([(k.t, one, s.t[:, j, :], j == 0, j == tiles - 1) for j in range(tiles)], ts, k.free)
                    s.free = [t]
                    t = a_act(z.t[:, :], k.t, ACT.Sqrt, t, t_e, z.free, bias=eps[:, :], scale=1.0 / (128 * tiles))
                    k.free = [t]
                    t = dve(lambda e, z=z: e.reciprocal(z.t[:, :], z.t[:, :]), t)
                    to = [d_stt(dst[:, j, 512 * ch:512 * ch + 512], r.t[:, j, :], v(vg + j), z.t[:, :], ALU.mult, ALU.mult, t)
                          for j in range(tiles)]
                    r.free = z.free = to
            w = load(5)
            t_K = []
            for ch in range(4):
                sl = slice(512 * ch, 512 * ch + 512)
                k, t = project(w.t, 64, 128, ch, w.ready)
                w.free = [t]
                r = ot[ch % 2]
                t = d_tt(r.t[64:128, :], k.t[64:128, :], CS[64:128, sl], ALU.mult, t, t_cs, r.free)
                k.free = [t]
                k = bank()
                t = mms([(k.t[64:128, :], cst[64:128, K_SEL:K_SEL + 64], r.t[64:128, :], True, True)], t, k.free)
                r.free = [t]
                t = [a_copy(KB[0].t[64:128, sl], k.t[64:128, :], t), a_copy(KB[1].t[64:128, sl], k.t[64:128, :])]
                k.free = t
                t_K += t
            for j in range(2):
                w = load(6 + j)
                for ch in range(4):
                    k, t = project(w.t, 0, 128, ch, w.ready)
                    w.free = [t]
                    k.free = [a_copy(qm[:, j, 512 * ch:512 * ch + 512], k.t, t)]
            for j in range(8):
                w = load(8 + j)
                for ch in range(4):
                    s, o = th2[ch % 2], ot[ch % 2]
                    k, t = project(w.t, 0, 128, ch, w.ready)
                    w.free = [t]
                    t1 = a_act(s.t[:, :], k.t, ACT.Tanh, t, s.free, scale=0.5)
                    t2 = d_stt(o.t[:, :], s.t[:, :], 1.0, k.t, ALU.add, ALU.mult, t1, o.free)
                    k.free = [t2]
                    s.free = [t2]
                    o.free = [dma(f"g4{ch % 2}", sp, feat("gT")[:, j, 512 * ch:512 * ch + 512], o.t[:, :], t2)]
                    stored.extend(o.free)
            st.close()
            P4.close()

            st = Stack()
            mT = st.sb("mT", [128, 8, 256])
            wm = st.sb("wm", [128, 8, 512])
            mi = [Buf(st.sb(f"mi{i}", [128, D])) for i in range(2)]
            mn = [Buf(st.sb(f"mn{i}", [128, D])) for i in range(2)]
            junk = st.sb("jm", [128, D])
            ss = st.sb("mss", [128, 6])
            t_wm = dma("wm", act, wm[:, :, :], A["w_mem"])
            tm = []
            tj = None
            for i in range(2):
                t = dma(f"mi{i}", sp, mi[i].t[:, :], A["mem"][128 * i:128 * i + 128, :])
                tj = a_act(junk[:, :], mi[i].t[:, :], ACT.Square, t, tj, acc=ss[:, i:i + 1])
                t2 = rsqrt(ss[:, 4 + i:5 + i], ss[:, i:i + 1], ss[:, 2 + i:3 + i], 1.0 / D, 1e-6, tj)
                t3 = d_ts(mn[i].t[:, :], mi[i].t[:, :], ss[:, 4 + i:5 + i], None, ALU.mult, None, t2)
                for j in range(2):
                    k = banks[2 * i + j]
                    t4 = mms([(k.t[:, 128 * q:128 * q + 128], mn[i].t[:, 512 * j + 128 * q:512 * j + 128 * q + 128], ident)
                              for q in range(4)], t3, k.free)
                    t5 = d_tt(mT[:, 4 * j:4 * j + 4, 128 * i:128 * i + 128], k.t.rearrange("p (a b) -> p a b", a=4),
                              spread(v(V_GM + 4 * j, 4), 128), ALU.mult, t4)
                    k.free = [t5]
                    tm.append(t5)
            t_m = []
            for j in range(2):
                k = banks[4 + j]
                t = mms([(k.t[:, 0:256], wm[:, q, 128 * j:128 * j + 128], mT[:, q, :], q == 0, q == 7) for q in range(8)],
                        tm, t_wm, k.free)
                k.free = [a_copy(kmT[:, j, :], k.t[:, 0:256], t)]
                t_m += k.free
                k = banks[6 + j]
                t = mms([(k.t[:, 0:256], mT[:, q, 128 * j:128 * j + 128], wm[:, q, 256:512], q == 0, q == 7) for q in range(8)],
                        k.free)
                k.free = [a_copy(vm[:, j, :], k.t[:, 0:256], t)]
                t_m += k.free
            st.close()

            st = Stack()
            w_v = st.sb("w_v", [128, 2, 768])
            V = st.sb("V2", [128, NT, 768])
            t_wv = dma("w_v", act, w_v[:, :, :], A["w_v"])
            t_V = []
            for i in range(NT):
                for n in range(2):
                    k = banks[(2 * i + n) % 8]
                    t = mms([(k.t[:, 0:384], ckv2[:, q, 128 * i:128 * i + 128], w_v[:, q, 384 * n:384 * n + 384], q == 0, q == 1)
                             for q in range(2)], t_wv, k.free)
                    cp = a_copy if n else d_copy
                    k.free = [cp(V[:, i, 384 * n:384 * n + 384], k.t[:, 0:384], t)]
                    t_V += k.free
            wq = [Buf(st.sb(f"wq{i}", [128, 3, 128])) for i in range(2)]
            wk = [Buf(st.sb(f"wk{i}", [128, 2, 64])) for i in range(2)]
            QB = [Buf(st.sb(f"QB{i}", [128, T])) for i in range(2)]
            Pb = [Buf(st.sb(f"P2{i}", [128, T])) for i in range(2)]
            pt = [Buf(st.sb(f"pt2{i}", [128, 512])) for i in range(4)]
            O = [Buf(st.sb(f"O{i}", [128, NT, 128])) for i in range(1)]
            g2 = [Buf(st.sb(f"g2{i}", [128, 512])) for i in range(2)]
            yo = [Buf(st.sb(f"y2{i}", [128, 512])) for i in range(2)]
            mx = [Buf(st.sb(f"mx2{i}", [128, 8])) for i in range(2)]
            sc = 1.0 / math.sqrt(96.0)
            PTB = [banks[4], banks[5]]
            OB = [banks[6], banks[7]]
            SB = banks[0:4]
            npt = [0]
            nx = [0]

            def head_load(h):
                a = h % 2
                wq[a].ready = [dma(f"wq{a}", sp, wq[a].t[:, :, :], A["w_uq2"][h], wq[a].free)]
                wk[a].ready = [dma(f"wk{a}", sp, wk[a].t[:, :, :], A["w_uk2"][h], wk[a].free)]

            def head_in(h):
                a, kf, qf = h % 2, KB[h % 2], QB[h % 2]
                qf.ready, kf.ready = [], []
                q0, k0 = qf.free, kf.free
                for ch in range(4):
                    sl = slice(512 * ch, 512 * ch + 512)
                    k = OB[1]
                    t = mms([(k.t, wq[a].t[:, q, :], cqT[:, q, sl], q == 0, q == 2) for q in range(3)], wq[a].ready, k.free)
                    wq[a].free = [t]
                    t = d_tt(qf.t[:, sl], k.t, CS[:, sl], ALU.mult, t, q0)
                    k.free = [t]
                    qf.ready.append(t)
                    yield
                    t = mms([(k.t[0:64, :], wk[a].t[:, q, :], ckv2[:, q, sl], q == 0, q == 1) for q in range(2)],
                            wk[a].ready, k.free)
                    wk[a].free = [t]
                    t = a_copy(kf.t[0:64, sl], k.t[0:64, :], t, k0)
                    k.free = [t]
                    kf.ready.append(t)
                    yield

            class Unit:

                def __init__(self, h, i, n):
                    self.h, self.i = h, i
                    self.p, self.m = Pb[n % 2], mx[n % 2]
                    self.tm, self.te, self.x = [], [], {}

                def qk(self, n):
                    kf, qf, m = KB[self.h % 2], QB[self.h % 2], self.m
                    t = mms([(SB[2 * n + j].t, qf.t[:, 128 * self.i:128 * self.i + 128],
                              kf.t[:, 1024 * n + 512 * j:1024 * n + 512 * j + 512], True, True) for j in range(2)],
                            SB[2 * n].free, qf.ready, kf.ready, t_K)
                    kf.free = qf.free = [t]
                    self.tm.append(dve(lambda e: e.tensor_reduce(m.t[:, n:n + 1], big[:, 1024 * n:1024 * n + 1024], AX, ALU.max),
                                       t, m.free))

                def exp(self):
                    p, m = self.p, self.m
                    t = d_ts(m.t[:, 2:3], m.t[:, 0:1], m.t[:, 1:2], -sc, ALU.max, ALU.mult, self.tm)
                    for n in range(2):
                        self.te.append(a_act(p.t[:, 1024 * n:1024 * n + 1024], big[:, 1024 * n:1024 * n + 1024], ACT.Exp,
                                             t, p.free, bias=m.t[:, 2:3], scale=sc, acc=m.t[:, 4 + n:5 + n]))
                        SB[2 * n].free = [self.te[-1]]

                def turn(self, c):
                    k, x = PTB[c % 2], pt[c]
                    t = mms([(k.t[:, 128 * j:128 * j + 128], self.p.t[:, 512 * c + 128 * j:512 * c + 128 * j + 128], ident)
                             for j in range(4)], self.te[c // 2], k.free)
                    cp = a_copy if c < 2 else d_copy
                    k.free = [cp(x.t[:, :], k.t, t, x.free)]
                    self.x[c] = k.free[0]
                    if c == 3:
                        self.p.free = [t]

                def pv(self, c):
                    ob, x, h, i, m = OB[0], pt[c], self.h, self.i, self.m
                    t = mms([(ob.t[:, 0:64], x.t[:, 128 * j:128 * j + 128], V[:, 4 * c + j, 64 * h:64 * h + 64],
                              c + j == 0, c + j == 6) for j in range(4)], self.x[c], t_V, ob.free)
                    x.free = [t]
                    if c == 3:
                        t1 = d_ts(m.t[:, 6:7], m.t[:, 4:5], m.t[:, 5:6], None, ALU.add, None, self.te)
                        t1 = dve(lambda e: e.reciprocal(m.t[:, 7:8], m.t[:, 6:7]), t1)
                        t1 = d_ts(O.t[:, i, 64 * (h % 2):64 * (h % 2) + 64], ob.t[:, 0:64], m.t[:, 7:8], None,
                                  ALU.mult, None, t, t1, ofree[i // 4])
                        ob.free = [t1]
                        m.free = [t1]
                        oready[i // 4].append(t1)

            O = O[0]
            ofree, oready = [[] for _ in range(4)], [[] for _ in range(4)]
            later = []

            def pair_out(j, ch):
                sl = slice(512 * ch, 512 * ch + 512)
                g, y = g2[ch % 2], yo[ch % 2]
                tg = dma(f"g2{ch % 2}", sp, g.t[:, :], feat("gT")[:, j, sl], g.free)
                while later:
                    later.pop()()
                k = OB[1]
                t = mms([(k.t[:, 128 * q:128 * q + 128], O.t[:, 4 * ch + q, :], ident) for q in range(4)],
                        oready[ch], k.free)
                ofree[ch], oready[ch] = [t], []
                t = d_stt(y.t[:, :], k.t, 0.5, g.t[:, :], ALU.mult, ALU.mult, t, tg, y.free)
                k.free = [t]
                g.free = [t]

                def store():
                    y.free = [dma(f"y2{ch % 2}", sp, feat("y2T")[:, j, sl], y.t[:, :], t)]
                    stored.extend(y.free)

                later.append(store)

            head_load(0)
            for _ in head_in(0):
                pass
            units = [(h, i) for h in range(12) for i in range(NT)]
            p1 = p2 = None
            hn = None
            for n in range(len(units) + 2):
                u = Unit(*units[n], n) if n < len(units) else None
                if u and u.i == 0:
                    if u.h < 11:
                        head_load(u.h + 1)
                        hn = head_in(u.h + 1)
                if u:
                    u.qk(0)
                if p2:
                    p2.pv(3)
                if p1:
                    p1.turn(0)
                if u:
                    u.qk(1)
                if p1:
                    p1.turn(1)
                if u:
                    u.exp()
                if p1:
                    p1.pv(0)
                    p1.turn(2)
                    p1.pv(1)
                    p1.turn(3)
                    p1.pv(2)
                if u and u.i % 2 and hn is not None:
                    next(hn, None)
                if u and u.i == 15 and hn is not None:
                    for _ in hn:
                        pass
                h, i = (n // NT, n % NT)
                if h and h % 2 == 0 and 1 <= i <= 4:
                    pair_out(h // 2 - 1, i - 1)
                p2, p1 = p1, u
            for ch in range(1, 4):
                pair_out(5, ch)

            msc = 0.125

            class Mem:
                def __init__(self, j, i):
                    self.j, self.i, self.b = j, i, i % 2

                def first(self):
                    j, i, b = self.j, self.i, self.b
                    kv = big[:, 1024 * b:1024 * b + 1024].rearrange("p (a b) -> p a b", a=2)[:, :, 0:256]
                    k, m, p = SB[2 * b], mx[b], Pb[b]
                    t = mms([(kv[:, e, :], qm[64 * e:64 * e + 64, j, 128 * i:128 * i + 128],
                              kmT[64 * e:64 * e + 64, j, :], True, True) for e in range(2)], k.free)
                    t = dve(lambda e: e.tensor_reduce(m.t[:, 0:2], kv, AX, ALU.max), t, m.free)
                    t = d_ts(m.t[:, 2:4], m.t[:, 0:2], -msc, None, ALU.mult, None, t)
                    self.te = [a_act(p.t[:, 256 * e:256 * e + 256], kv[:, e, :], ACT.Exp, t, p.free,
                                     bias=m.t[:, 2 + e:3 + e], scale=msc, acc=m.t[:, 4 + e:5 + e]) for e in range(2)]
                    k.free = self.te
                    self.tr = dve(lambda e: e.reciprocal(m.t[:, 6:8], m.t[:, 4:6]), self.te)

                def second(self):
                    b, p = self.b, Pb[self.b]
                    k, x = PTB[b], pt[b]
                    t = mms([(k.t[:, 128 * q:128 * q + 128], p.t[:, 128 * q:128 * q + 128], ident) for q in range(4)],
                            self.te, k.free)
                    p.free = [t]
                    k.free = [a_copy(x.t[:, :], k.t, t, x.free)]
                    self.x = k.free

                def third(self):
                    j, i, b = self.j, self.i, self.b
                    ob, x, m = OB[0], pt[b], mx[b]
                    t = mms([(ob.t[:, 64 * e:64 * e + 64], x.t[:, 256 * e + 128 * q:256 * e + 128 * q + 128],
                              vm[:, q, 128 * j + 64 * e:128 * j + 64 * e + 64], q == 0, q == 1)
                             for e in range(2) for q in range(2)], self.x, ob.free)
                    x.free = [t]
                    t = d_tt(O.t[:, i, :].rearrange("p (a b) -> p a b", a=2), ob.t[:, 0:128].rearrange("p (a b) -> p a b", a=2),
                             spread(m.t[:, 6:8], 64), ALU.mult, t, self.tr, ofree[i // 4])
                    ob.free = [t]
                    m.free = [t]
                    oready[i // 4].append(t)

            tiles = [(j, i) for j in range(2) for i in range(NT)]
            p1 = p2 = None
            for n in range(len(tiles) + 2):
                u = Mem(*tiles[n]) if n < len(tiles) else None
                if p2:
                    p2.third()
                if u:
                    u.first()
                if p1:
                    p1.second()
                if p2 and p2.i % 4 == 3:
                    pair_out(6 + p2.j, p2.i // 4)
                p2, p1 = p1, u
            while later:
                later.pop()()
            st.close()
            P5.close()

        def phase6():
            st = Stack()

            def done(i, g, t):
                ts = dma(f"out{i % 2}", sp, A["out"][128 * i:128 * i + 128, :], g.t[:, :], t)
                stored.append(ts)
                g.free = [ts]

            mix_out(st, st.sb, "m2", "y2T", A["w_out2"], scratch["x1"], A["final_g2"], done)
            st.close()

        if upto == 3:
            P4, hT, _ = phase3()
            P4.close()
        if upto >= 5:
            phase45()
        if upto >= 6:
            phase6()
        sp.after(stored)
        sp.after(now())

        with nc.Block() as block:
            @block.sync
            def _(e):
                sp.emit(e)

            @block.scalar
            def _(e):
                act.emit(e)

            @block.vector
            def _(e):
                dve.emit(e)

            @block.tensor
            def _(e):
                pe.emit(e)

            @block.gpsimd
            def _(e):
                pool.emit(e)


def constants():
    c = np.zeros((128, K_N), np.float32)
    r = np.arange(128)
    c[:, K_ID:K_ID + 128] = np.eye(128)
    c[:, K_BLK:K_BLK + 128] = (r[:, None] // 64) == (r[None, :] // 64)
    c[:, K_ONE:K_ONE + 128] = 1.0
    s, t = (r % 64)[:, None], np.arange(64)[None, :]
    c[:, K_GM:K_GM + 64] = s < t
    c[:, K_GM + 64:K_GM + 128] = s <= t
    same = (r[:, None] // 64) == (r[None, :] // 64)
    a, b = (r % 64)[:, None], (r % 64)[None, :]
    for i in range(6):
        m = 1 << i
        c[:, K_LV + 128 * i:K_LV + 128 * i + 128] = same & (a // m % 2 == 0) & (b // m == a // m + 1)
    c[:, K_RS:K_RS + UT] = (np.arange(UT) % C != 0)[None, :]
    c[:, K_SEL:K_SEL + 64] = (r[:, None] % 32) == (np.arange(64)[None, :] % 32)
    c[:, K_NEG:K_NEG + 16] = -0.5
    inv = (np.float32(1.0) / (np.float32(10000.0) ** (np.arange(0, 32, 2, dtype=np.float32) / np.float32(32)))).astype(np.float32)
    c[64:128, K_INV] = np.tile(inv, 4)
    c[64:96, K_PH] = 0.25
    c[:, K_SGN] = 1.0
    c[96:112, K_SGN] = -1.0
    return c


def arrange(inp):
    g = {k: np.asarray(a) for k, a in inp.items()}
    f = np.ascontiguousarray

    def cols(x):
        return x.reshape(-1, 128).T

    w_in = g["w_in"][0]

    def tile(w, c):
        return w[:, c].reshape(8, 128, len(c)).transpose(1, 0, 2)

    vec = np.zeros((128, V_N), np.float32)
    vec[:, V_G1:V_G1 + 8] = cols(g["norm_g"][0])
    mu = g["mu_shift"][0]
    for hp in range(4):
        for j in range(3):
            vec[:, V_MU + 3 * hp + j] = mu[512 * j + 128 * hp:512 * j + 128 * hp + 128]
    vec[0:64, V_MUL] = mu[1536:1600]
    for o, n in ((V_W0, "w0"), (V_A0, "a0"), (V_KK, "k_k"), (V_KA, "k_a"), (V_RK, "r_k"), (V_GG, "gn_g"), (V_GB, "gn_b")):
        vec[:, o:o + 4] = cols(g[n][0].reshape(-1))
    vec[:, V_QN:V_QN + 2] = cols(g["q_norm_g"][0])
    vec[:, V_KVN] = g["kv_norm_g"][0]
    vec[:, V_IG] = np.tile(g["kidx_g"][0], 2)
    vec[:, V_IB] = np.tile(g["kidx_b"][0], 2)
    vec[:, V_G2:V_G2 + 8] = cols(g["norm_g_l0_2"])
    vec[:, V_QN2:V_QN2 + 3] = cols(g["q_norm_g_l0_2"])
    vec[:, V_KVN2:V_KVN2 + 2] = cols(g["kv_norm_g_l0_2"])
    vec[:, V_GM:V_GM + 8] = cols(g["mem_norm_g_l0_2"])

    r = np.arange
    pre = [r(2112, 2240), r(2240, 2368), r(2368, 2496), np.concatenate([r(2496, 2560)] * 2)]
    pre += [r(2564 + 128 * j, 2692 + 128 * j) for j in range(4)]
    rw = [r(o + 128 * hp, o + 128 * hp + 128) for hp in range(4) for o in (0, 512, 1024, 1600)]
    w2 = g["w_in_l0_2"]
    rope = r(640, 672)
    swap = np.concatenate([rope[16:], rope[:16]])
    in2 = [r(128 * j, 128 * j + 128) for j in range(5)] + [np.concatenate([rope, swap, rope, swap])]
    in2 += [r(672 + 128 * j, 800 + 128 * j) for j in range(10)]
    uq = g["w_uq_l0_2"].reshape(3, 128, 12, 96)
    uq = np.concatenate([uq, uq[..., 80:96], uq[..., 64:80]], axis=-1).transpose(2, 1, 0, 3)
    ukv = g["w_ukv_l0_2"].reshape(2, 128, 12, 128)
    wuk = np.zeros((128, 8, 128), np.float32)
    for h in range(8):
        wuk[64 * (h % 2):64 * (h % 2) + 64, h, :] = g["w_uk"][0][h].T
    low = np.zeros((64, 2, 512), np.float32)
    low[0:32, 0], low[32:64, 1] = g["w_up"][0], g["a_up"][0]
    return {
        "cst": constants(), "vec": vec,
        "x": g["x"][0], "mem": g["mem_2"][0], "pos": f(np.broadcast_to(g["positions_2"], (64, T))),
        "w_pre": f(np.stack([tile(w_in, c) for c in pre])),
        "w_rw": f(np.stack([tile(w_in, c) for c in rw])),
        "w_l": f(tile(w_in, r(1536, 1600))), "w_x": f(tile(w_in, r(2560, 2564))),
        "w_uq": f(g["w_uq"][0].reshape(2, 128, 512).transpose(1, 0, 2)),
        "w_qi": f(g["w_qidx"][0].reshape(2, 128, 256).transpose(1, 0, 2)),
        "w_uk": wuk, "w_uv": f(g["w_uv"][0].transpose(1, 0, 2)),
        "w_lo": low,
        "w_out": f(g["w_out"][0].reshape(8, 128, D)), "final_g": f(np.broadcast_to(g["final_g"], (128, D))),
        "w_in2": f(np.stack([tile(w2, c) for c in in2])),
        "w_uq2": f(uq), "w_uk2": f(ukv[..., 0:64].transpose(2, 1, 0, 3)),
        "w_v": f(ukv[..., 64:128].reshape(2, 128, 768).transpose(1, 0, 2)),
        "w_mem": f(g["w_mem_kv_l0_2"].reshape(8, 128, 512).transpose(1, 0, 2)),
        "w_out2": f(g["w_out_l0_2"].reshape(8, 128, D)), "final_g2": f(np.broadcast_to(g["final_norm_g_2"], (128, D))),
    }


def kernel(**inputs):
    import concourse.bacc as _bacc
    from concourse.bass_utils import run_bass_kernel_spmd as _run

    nc = _bacc.Bacc("TRN2", target_bir_lowering=False, num_devices=1)
    arrays = arrange(inputs)
    A = {k: nc.dram_tensor("in_" + k, a.shape, mybir.dt.from_np(a.dtype), kind="ExternalInput").ap()
         for k, a in arrays.items()}
    A["out"] = nc.dram_tensor("out_0", (T, D), F32, kind="ExternalOutput").ap()
    program(nc, A)
    r = _run(nc, [{"in_" + k: a for k, a in arrays.items()}], core_ids=[0])
    return r.results[0]["out_0"].reshape(1, T, D)
```
